# Optimizing a Trainium2 kernel written in Bass

```python
import jax
import jax.numpy as jnp
from jax import lax
import numpy as np

D_MODEL = 1024
BATCH = 1
SEQ = 1024
DEPTH = 1

CHUNK = 64
D_MIX = D_MODEL
HEAD_DIM = 64
D_A = D_MIX // 2
D_B = D_MIX - D_A
N_HEADS_A = D_A // HEAD_DIM
N_HEADS_B = D_B // HEAD_DIM
N_IDX_HEADS = 16
IDX_DIM = 64
TOPK_MAX = 256
ROPE_THETA = 500000.0
ROT_DIM = HEAD_DIM // 4
IDX_ROT_DIM = IDX_DIM // 4
RET_THETA = 10000.0
Q_BLOCK = 128
N_GROUPS = 4
EXPERTS_PER_GROUP = 8
N_EXPERTS = N_GROUPS * EXPERTS_PER_GROUP
TOP_K_FINE = 2
D_EXPERT = D_MODEL // 2
MOE_BLOCK = 128
EPS = 1e-6
SPLITS = (D_A, D_A, D_A, N_IDX_HEADS * IDX_DIM, IDX_DIM, N_IDX_HEADS, D_B, D_B, D_B, D_B)
D_IN = sum(SPLITS)

kernel_name = 'hybrid_dsa_retention_hmoe_block'

def rmsnorm(x, g):
    xf = x.astype(jnp.float32)
    xf = xf * lax.rsqrt(jnp.mean(xf * xf, axis=-1, keepdims=True) + EPS)
    return xf.astype(x.dtype) * g

def rope(x, pos, rot_dim, theta):
    half = rot_dim // 2
    inv_freq = theta ** (-jnp.arange(half, dtype=jnp.float32) / half)
    ang = pos.astype(jnp.float32)[:, :, None, None] * inv_freq
    cos, sin = jnp.cos(ang), jnp.sin(ang)
    xr = x[..., :rot_dim].astype(jnp.float32)
    x1, x2 = xr[..., :half], xr[..., half:]
    rot = jnp.concatenate([x1 * cos - x2 * sin, x2 * cos + x1 * sin], axis=-1).astype(x.dtype)
    return jnp.concatenate([rot, x[..., rot_dim:]], axis=-1)

def dsa_attention(q, k, v, q_idx, k_idx, w_idx):
    B, S = q.shape[0], q.shape[1]
    k_top = min(TOPK_MAX, S // 4)
    n_blk = S // Q_BLOCK
    key_chunk = jnp.arange(S) // CHUNK

    def to_blocks(t):
        return t.reshape((B, n_blk, Q_BLOCK) + t.shape[2:]).swapaxes(0, 1)

    def block(xs):
        i, qb, qib, wb = xs
        q_chunk = (i * Q_BLOCK + jnp.arange(Q_BLOCK)) // CHUNK
        dots = jnp.einsum('bqhe,bse->bqhs', qib, k_idx, preferred_element_type=jnp.float32)
        score = jnp.einsum('bqh,bqhs->bqs', wb.astype(jnp.float32), jax.nn.relu(dots * IDX_DIM ** -0.5))
        admissible = key_chunk[None, :] <= q_chunk[:, None]
        score = jnp.where(admissible[None], score, -jnp.inf)
        _, sel = lax.top_k(score, k_top)
        k_sel = jax.vmap(lambda kk, ii: kk[ii])(k, sel)
        v_sel = jax.vmap(lambda vv, ii: vv[ii])(v, sel)
        valid = key_chunk[sel] <= q_chunk[None, :, None]
        logits = jnp.einsum('bqhd,bqkhd->bqhk', qb, k_sel, preferred_element_type=jnp.float32) * HEAD_DIM ** -0.5
        logits = jnp.where(valid[:, :, None, :], logits, -1e30)
        p = jax.nn.softmax(logits, axis=-1).astype(v.dtype)
        return jnp.einsum('bqhk,bqkhd->bqhd', p, v_sel)

    out = lax.map(block, (jnp.arange(n_blk), to_blocks(q), to_blocks(q_idx), to_blocks(w_idx)))
    return out.swapaxes(0, 1).reshape(B, S, -1)

def retention(q, k, v, g, pos):
    B, S, H, d = q.shape
    n_c = S // CHUNK
    dt = v.dtype
    log_gamma = jnp.log1p(-jnp.exp2(-5.0 - jnp.arange(H, dtype=jnp.float32)))
    q = rope(q, pos, d, RET_THETA).astype(jnp.float32).reshape(B, n_c, CHUNK, H, d)
    k = (rope(k, pos, d, RET_THETA).astype(jnp.float32) * d ** -0.5).reshape(B, n_c, CHUNK, H, d)
    v = v.astype(jnp.float32).reshape(B, n_c, CHUNK, H, d)
    n = jnp.arange(CHUNK, dtype=jnp.float32)
    diff = n[:, None] - n[None, :]
    decay = jnp.where(diff[None] >= 0, jnp.exp(jnp.maximum(diff, 0.0)[None] * log_gamma[:, None, None]), 0.0)
    scores = jnp.einsum('bcnhd,bcmhd->bchnm', q, k) * decay
    inner = jnp.einsum('bchnm,bcmhe->bcnhe', scores, v)
    zeta = jnp.exp((CHUNK - 1.0 - n)[:, None] * log_gamma[None, :])
    kv = jnp.einsum('bcmhd,bcmhe->bchde', k * zeta[None, None, :, :, None], v)
    g_chunk = jnp.exp(CHUNK * log_gamma)[None, :, None, None]

    def step(state, kv_c):
        return state * g_chunk + kv_c, state

    _, prev = lax.scan(step, jnp.zeros((B, H, d, d), jnp.float32), kv.swapaxes(0, 1))
    prev = prev.swapaxes(0, 1)
    xi = jnp.exp((n + 1.0)[:, None] * log_gamma[None, :])
    cross = jnp.einsum('bcnhd,bchde->bcnhe', q, prev) * xi[None, None, :, :, None]
    y = (inner + cross).reshape(B, S, H, d)
    mu = jnp.mean(y, axis=-1, keepdims=True)
    var = jnp.mean(jnp.square(y - mu), axis=-1, keepdims=True)
    y = (y - mu) * lax.rsqrt(var + EPS)
    return (jax.nn.silu(g.astype(jnp.float32)) * y).astype(dt).reshape(B, S, H * d)

def hybrid_mixer(h, positions, w_in, w_o):
    B, S, _ = h.shape
    proj = jnp.einsum('bsd,de->bse', h, w_in)
    cuts = [int(i) for i in np.cumsum(SPLITS)[:-1]]
    qa, ka, va, qi, ki, wi, qb, kb, vb, gb = jnp.split(proj, cuts, axis=-1)
    qa = rope(qa.reshape(B, S, N_HEADS_A, HEAD_DIM), positions, ROT_DIM, ROPE_THETA)
    ka = rope(ka.reshape(B, S, N_HEADS_A, HEAD_DIM), positions, ROT_DIM, ROPE_THETA)
    va = va.reshape(B, S, N_HEADS_A, HEAD_DIM)
    qi = rope(qi.reshape(B, S, N_IDX_HEADS, IDX_DIM), positions, IDX_ROT_DIM, ROPE_THETA)
    ki = rope(ki.reshape(B, S, 1, IDX_DIM), positions, IDX_ROT_DIM, ROPE_THETA)[:, :, 0]
    wi = wi * N_IDX_HEADS ** -0.5
    y_a = dsa_attention(qa, ka, va, qi, ki, wi)
    shp = (B, S, N_HEADS_B, HEAD_DIM)
    y_b = retention(qb.reshape(shp), kb.reshape(shp), vb.reshape(shp), gb.reshape(shp), positions)
    y = jnp.concatenate([y_a, y_b], axis=-1)
    return jnp.einsum('bse,ed->bsd', y, w_o)

def hier_moe(h, w_router_group, w_router_expert, w_up, w_gate, w_down):
    B, S, D = h.shape
    tok = h.reshape(-1, D)
    N = tok.shape[0]
    pg = jax.nn.softmax(jnp.einsum('nd,dg->ng', tok, w_router_group).astype(jnp.float32), axis=-1)
    grp = jnp.argmax(pg, axis=-1)
    p_grp = jnp.max(pg, axis=-1)
    fine = jnp.einsum('nd,gde->nge', tok, w_router_expert).astype(jnp.float32)
    fine = jnp.take_along_axis(fine, grp[:, None, None], axis=1)[:, 0]
    pe = jax.nn.softmax(fine, axis=-1)
    top_p, top_i = lax.top_k(pe, TOP_K_FINE)
    weights = p_grp[:, None] * top_p / jnp.sum(top_p, axis=-1, keepdims=True)
    experts = grp[:, None] * EXPERTS_PER_GROUP + top_i
    A = N * TOP_K_FINE
    e_flat = experts.reshape(-1)
    w_flat = weights.reshape(-1)
    t_flat = jnp.repeat(jnp.arange(N), TOP_K_FINE)
    order = jnp.argsort(e_flat)
    e_s, t_s, w_s = e_flat[order], t_flat[order], w_flat[order]
    counts = jnp.bincount(e_flat, length=N_EXPERTS)
    starts = jnp.cumsum(counts) - counts
    padded = (counts + MOE_BLOCK - 1) // MOE_BLOCK * MOE_BLOCK
    pends = jnp.cumsum(padded)
    pstarts = pends - padded
    dest = pstarts[e_s] + (jnp.arange(A) - starts[e_s])
    P = A + N_EXPERTS * MOE_BLOCK
    n_blocks = P // MOE_BLOCK
    x_buf = jnp.zeros((P, D), h.dtype).at[dest].set(tok[t_s])
    w_buf = jnp.zeros((P,), jnp.float32).at[dest].set(w_s)
    t_buf = jnp.zeros((P,), jnp.int32).at[dest].set(t_s.astype(jnp.int32))
    blk_expert = jnp.minimum(jnp.searchsorted(pends, jnp.arange(n_blocks) * MOE_BLOCK, side='right'), N_EXPERTS - 1)

    def run(xs):
        xb, e = xs
        return (jax.nn.silu(xb @ w_gate[e]) * (xb @ w_up[e])) @ w_down[e]

    y_buf = lax.map(run, (x_buf.reshape(n_blocks, MOE_BLOCK, D), blk_expert)).reshape(P, D)
    out = jnp.zeros((N, D), h.dtype).at[t_buf].add(y_buf * w_buf[:, None].astype(h.dtype))
    return out.reshape(B, S, D)

def setup_inputs(seed: int = 0) -> dict:
    key = jax.random.key(seed)
    ks = jax.random.split(key, 16)
    nrm = jax.random.normal
    D = D_MODEL
    x = nrm(ks[0], (BATCH, SEQ, D), jnp.float32)
    c = nrm(ks[1], (BATCH, D), jnp.float32)
    offs = jax.random.randint(ks[2], (BATCH, 1), 0, 4096)
    positions = (offs + jnp.arange(SEQ)[None, :]).astype(jnp.int32)
    w_ada = nrm(ks[3], (DEPTH, D, 6 * D), jnp.float32) * (0.5 * D ** -0.5)
    b_ada = 0.01 * nrm(ks[4], (DEPTH, 6 * D), jnp.float32)
    g_norm_mix = 1.0 + 0.01 * nrm(ks[5], (DEPTH, D), jnp.float32)
    w_in = nrm(ks[6], (DEPTH, D, D_IN), jnp.float32) * D ** -0.5
    w_o = nrm(ks[7], (DEPTH, D_MIX, D), jnp.float32) * D_MIX ** -0.5
    g_norm_ffn = 1.0 + 0.01 * nrm(ks[8], (DEPTH, D), jnp.float32)
    w_router_group = nrm(ks[9], (DEPTH, D, N_GROUPS), jnp.float32) * D ** -0.5
    w_router_expert = nrm(ks[10], (DEPTH, N_GROUPS, D, EXPERTS_PER_GROUP), jnp.float32) * D ** -0.5
    w_up = nrm(ks[11], (DEPTH, N_EXPERTS, D, D_EXPERT), jnp.float32) * D ** -0.5
    w_gate = nrm(ks[12], (DEPTH, N_EXPERTS, D, D_EXPERT), jnp.float32) * D ** -0.5
    w_down = nrm(ks[13], (DEPTH, N_EXPERTS, D_EXPERT, D), jnp.float32) * D_EXPERT ** -0.5
    g_norm_final = 1.0 + 0.01 * nrm(ks[14], (D,), jnp.float32)
    return {'x': x, 'c': c, 'positions': positions, 'w_ada': w_ada, 'b_ada': b_ada,
            'g_norm_mix': g_norm_mix, 'w_in': w_in, 'w_o': w_o, 'g_norm_ffn': g_norm_ffn,
            'w_router_group': w_router_group, 'w_router_expert': w_router_expert,
            'w_up': w_up, 'w_gate': w_gate, 'w_down': w_down, 'g_norm_final': g_norm_final}

def reference(x, c, positions, w_ada, b_ada, g_norm_mix, w_in, w_o, g_norm_ffn,
              w_router_group, w_router_expert, w_up, w_gate, w_down, g_norm_final):
    for l in range(DEPTH):
        mod = jnp.einsum('bd,de->be', c, w_ada[l]) + b_ada[l]
        sh1, sc1, gt1, sh2, sc2, gt2 = jnp.split(mod, 6, axis=-1)
        h = rmsnorm(x, g_norm_mix[l]) * (1.0 + sc1[:, None, :]) + sh1[:, None, :]
        x = x + gt1[:, None, :] * hybrid_mixer(h, positions, w_in[l], w_o[l])
        h = rmsnorm(x, g_norm_ffn[l]) * (1.0 + sc2[:, None, :]) + sh2[:, None, :]
        x = x + gt2[:, None, :] * hier_moe(h, w_router_group[l], w_router_expert[l], w_up[l], w_gate[l], w_down[l])
    return rmsnorm(x, g_norm_final)


_drawn_inputs = setup_inputs


def setup_inputs(seed=0):
    import zlib

    import numpy as np

    out = dict(_drawn_inputs(seed))
    spreads = {}
    factors = {'g_norm_mix': 3.696, 'g_norm_ffn': 3.459, 'g_norm_final': 5.791}
    for name, (base, spread) in spreads.items():
        noise = np.random.default_rng([zlib.crc32(name.encode()), seed]).standard_normal(out[name].shape)
        drawn = base * np.exp(spread * noise) if base else spread * noise
        out[name] = jnp.asarray(drawn.astype(out[name].dtype))
    for name, factor in factors.items():
        out[name] = (out[name] * factor).astype(out[name].dtype)
    return out
```

```python
from contextlib import ExitStack

import numpy as np
import concourse.bass as bass
from concourse import mybir

F32 = mybir.dt.float32
I32 = mybir.dt.int32
ALU = mybir.AluOpType
ACT = mybir.ActivationFunctionType
X_AXIS = mybir.AxisListType.X

P = 128
D = 1024
S = 1024
T = S // P
KD = D // P
HD = 64
HA, HB = 8, 8
NIH = 16
TOPK = 256
DMIX = 512
NG, EPG = 4, 8
NE = NG * EPG
FE = 512
KF = FE // P
EPS = 1e-6
D_IN = 4688
MAX_ITEMS = 2 * S // P + NE
TBL = MAX_ITEMS + 2
NEG_SCORE = -3.0e38
B_SPEND = (8.0, 8.0, 8.0)
TAKEN = -3.4e38
NEG_LOGIT = -1.0e30
ROUND = 12582912.0
TWO_PI = 2.0 * np.pi
PI_HI = 6.28125
PI_MID = float(np.float32(np.round((TWO_PI - PI_HI) * 2**20) / 2**20))
PI_LO = float(np.float32(TWO_PI - PI_HI - PI_MID))
PI_IN = 3.1415925

CHUNKS_A = (("qi0", 1536, 512), ("qi1", 2048, 512), ("kiwi", 2560, 80), ("qa", 0, 512),
            ("ka", 512, 512), ("va", 1024, 512))
NA1 = 3
CHUNKS_B = (("qb", 2640), ("kb", 3152), ("vb", 3664), ("gb", 4176))
FIRST_SCORED = TOPK // P
SCORED = range(FIRST_SCORED, T)
ACC_OFF = {i: sum(P * (j + 1) for j in SCORED if j < i) for i in SCORED}
ACC_ALL = sum(P * (j + 1) for j in SCORED)


def constant_table():
    p = np.arange(P)
    parts = {}
    parts["ident"] = np.eye(P)
    parts["before"] = (p[:, None] < p[None, :])
    parts["causal"] = (p[None, :] >= p[:, None])
    inv_a = np.float32(500000.0) ** (-np.arange(8, dtype=np.float32) / np.float32(8))
    inv_b = np.float32(10000.0) ** (-np.arange(32, dtype=np.float32) / np.float32(32))
    parts["invf"] = np.tile(np.concatenate([inv_a, inv_b])[None], (P, 1))
    lg = np.log1p(-np.exp2(-5.0 - np.arange(HB)))
    parts["kfac"] = np.exp(-(p[:, None] + 1.0) * lg[None]) * HD ** -0.5
    parts["xi"] = np.exp((p[:, None] + 1.0) * lg[None])
    parts["carry"] = np.tile(np.repeat(np.exp(P * lg), HD)[None], (P, 1))
    parts["unseen"] = np.tile(np.where(p < HD, 1.0, 0.0)[:, None], (1, HD))
    parts["desc"] = np.tile(np.arange(8, 0, -1)[None], (P, 1))
    parts["iota"] = np.tile(np.arange(P)[None], (P, 1))
    parts["even"] = np.tile(2 * np.arange(MAX_ITEMS // 2)[None], (P, 1))
    parts["token"] = p[:, None] + P * np.arange(T)[None]
    at, off = {}, 0
    for name, a in parts.items():
        at[name] = (off, off + a.shape[1])
        off += a.shape[1]
    return np.ascontiguousarray(np.concatenate([np.asarray(a, np.float32) for a in parts.values()], 1)), at


CONST, CONST_AT = constant_table()


class Own:

    def __init__(self, engine, step):
        self.engine, self.step, self.count = engine, step, {}
        self.last = None

    def go(self, instruction, sem=None):
        sem = sem or self.step
        instruction.then_inc(sem, 1)
        self.count[sem.name] = self.count.get(sem.name, 0) + 1
        self.last = (sem, self.count[sem.name])

    def wait(self):
        self.engine.wait_ge(*self.last)

    def __call__(self, instruction, sem=None):
        self.go(instruction, sem)
        self.wait()


def block_kernel(nc, x, ccol, pos, w_ada, b_cols, b_gt1, b_gt2, g_cols, g_final, w_in, w_o, w_router,
                 w_up, w_gate, w_down, const, out):
    ctx = ExitStack()
    with ctx:
        def sb(name, shape, dt=F32):
            return ctx.enter_context(nc.sbuf_tensor(name, shape, dt))

        def sem(name):
            return ctx.enter_context(nc.semaphore(name))

        def sems(name, n):
            return [sem(f"{name}{i}") for i in range(n)]

        q_dram = nc.dram_tensor("q_dram", (P, 4, S), F32).ap()
        yb_dram = nc.dram_tensor("yb_dram", (S, DMIX), F32).ap()
        x1_dram = nc.dram_tensor("x1_dram", (S, D), F32).ap()
        xn_dram = nc.dram_tensor("xn_dram", (S, D), F32).ap()
        y_dram = nc.dram_tensor("y_dram", (MAX_ITEMS * P, D), F32).ap()

        BIG = sb("BIG", [P, 24576])
        hT = BIG[:, 0:8192].rearrange("p (k s) -> p k s", k=KD)
        ring = [BIG[:, 8192 + 4096 * i:8192 + 4096 * (i + 1)].rearrange("p (k c) -> p k c", k=KD) for i in range(2)]
        qiT = BIG[:, 16384:24576].rearrange("p (j s) -> p j s", j=8)
        ada_slot = [BIG[:, 0:8192].rearrange("p (k c) -> p k c", k=KD),
                    BIG[:, 16384:24576].rearrange("p (k c) -> p k c", k=KD)]
        ada_late = [BIG[:, 0:8192].rearrange("p (k c) -> p k c", k=KD),
                    BIG[:, 16384:24576].rearrange("p (k c) -> p k c", k=KD)]
        wb = [ring[0], ring[1],
              BIG[:, 16384:20480].rearrange("p (k c) -> p k c", k=KD),
              BIG[:, 20480:24576].rearrange("p (k c) -> p k c", k=KD)]
        wo = BIG[:, 8192:16384].rearrange("p (k c) -> p k c", k=KD)
        wg = [BIG[:, 12288 * s:12288 * s + 4096].rearrange("p (k f) -> p k f", k=KD) for s in range(2)]
        wu = [BIG[:, 12288 * s + 4096:12288 * s + 8192].rearrange("p (k f) -> p k f", k=KD) for s in range(2)]
        wd = [BIG[:, 12288 * s + 8192:12288 * s + 12288].rearrange("p (k f) -> p k f", k=KF) for s in range(2)]

        KV = sb("KV", [P, 8192 + 2048])
        kaT = KV[:, 0:4096].rearrange("p (j s) -> p j s", j=4)
        va = KV[:, 4096:8192].rearrange("p (t c) -> p t c", t=T)
        kiBD = KV[:, 8192:10240].rearrange("p (h s) -> p h s", h=2)
        xall = KV[:, 0:8192].rearrange("p (t d) -> p t d", t=T)
        ACC = sb("ACC", [P, ACC_ALL])
        cst = sb("cst", [P, CONST.shape[1]])
        ones = sb("ones", [P, P])
        WK = sb("WK", [P, 10000])

        def c(name):
            a, b = CONST_AT[name]
            return cst[:, a:b]

        ident = c("ident")
        cc = sb("cc", [P, KD])
        bc = sb("bc", [P, 4, KD])
        gc = sb("gc", [P, 2, KD])
        mod = sb("mod", [P, 4, KD])
        posi = sb("posi", [P, T], I32)
        posf = sb("posf", [P, T])
        tab = sb("tab", [P, 3, T, 40])
        wsc = sb("wsc", [P, T, NIH])
        zero = sb("zero", [P, 512])
        small = sb("small", [P, 64])
        expo = sb("expo", [P, 8])
        L = sb("L", [P, T, 36])

        cosT, sinT, nsinT = tab[:, 0], tab[:, 1], tab[:, 2]

        def work(spec):
            out_, off = {}, 0
            for name, shape in spec:
                n = int(np.prod(shape))
                v = WK[:, off:off + n]
                if len(shape) == 2:
                    v = v.rearrange("p (a b) -> p a b", a=shape[0])
                elif len(shape) == 3:
                    v = v.rearrange("p (a b c) -> p a b c", a=shape[0], b=shape[1])
                out_[name] = v
                off += n
            assert off <= 10000, off
            return out_

        W0 = work([("sq", (D,)), ("dg", (512,)), ("ang", (T, 40)), ("k", (T, 40)), ("r", (T, 40)), ("c", (T, 40))])
        WA = work([("tmp", (3, 512)), ("s1", (128,)), ("s2", (128,)), ("trq", (2, 512)), ("R", (3, 1024))])
        WB = work([("qA", (2, 512)), ("kA", (2, 512)), ("qB", (512,)), ("kB", (512,)), ("v", (2, 512)),
                   ("g", (2, 512)), ("qBD", (4, 2, P)), ("kT", (4, P)), ("st", (4, P)),
                   ("y", (2, 512)), ("sq", (512,))])
        WB["S"] = KV[:, 8192:9216].rearrange("p (h n) -> p h n", h=HB)
        Wk = KV[:, 9216:10240]
        m8 = sb("m8", [P, 8])[:, :]
        WC = work([("q", (2, 1024)), ("S", (3, 1024)), ("PT", (2, 512)),
                   ("y", (512,)), ("yb", (512,)), ("yT", (8, P)), ("bias01", (256,)), ("wr", (8 * 36,)),
                   ("sq", (D,))])
        WC["gt1"] = KV[:, 8192:9216]
        WC["qBD"] = [WC["q"][:, s].rearrange("p (j h n) -> p j h n", j=4, h=2) for s in range(2)]
        WC["x"] = KV[:, 9216:10240]
        WC["h2T"] = WC["yT"]
        gt2 = KV[:, 0:D]
        WR = work([("e1", (T, NE)), ("e2", (T, NE)), ("A", (T, NE)), ("pre", (T, NE)), ("V", (T, NE)),
                   ("tmp", (T, NE)), ("f", (T, 8)), ("f2", (T, 8)), ("o1", (T, 8)), ("o2", (T, 8)),
                   ("ca", (T, 8)), ("G", (T, NG)), ("cg", (T, NG)), ("m", (T,)), ("gm", (T,)), ("t1", (T,)),
                   ("t2", (T,)), ("e2x", (T,)), ("cnt", (NE,)), ("nb", (NE,)), ("ends", (2, NE)), ("start", (NE,)),
                   ("row", (2, T)), ("q", (2, T)), ("r", (2, T)), ("h48", (48,)), ("it", (MAX_ITEMS * NE,)),
                   ("ohp", (2, P)), ("ohi", (2, 64)), ("ef", (64,)), ("h", (64,))])
        WM = work([("Xg", (2, D)), ("xT", (2, KD, P)), ("h", (2, FE)), ("hs", (FE,)), ("hT", (2, KF, P)),
                   ("Y", (2, D))])
        WF = work([("x", (2, D)), ("y1", (2, D)), ("y2", (2, D)), ("gf", (D,)), ("sq", (D,))])
        sw = sb("sw", [P, 2, T])
        srow = sb("srow", [P, 2, T], I32)
        tbl = sb("tbl", [P, TBL], I32)
        gidx = sb("gidx", [P, 2], I32)
        ssum = sb("ssum", [P, 2, 8])
        nmax = sb("nmax", [P, 4])
        items = sb("items", [1, 64], I32)

        PS = ctx.enter_context(nc.psum_tensor("PS", [P, 8, 512], F32))

        class Signals:

            def __init__(self):
                self.made = {}

            def __call__(self, name):
                if name not in self.made:
                    self.made[name] = sem(name)
                return self.made[name]

        G = Signals()
        wada_v = w_ada.rearrange("(k p) (a c) -> p a k c", p=P, a=6)
        win_v = w_in.rearrange("(k p) c -> p k c", p=P)
        wo_v = w_o.rearrange("(k p) c -> p k c", p=P)
        x_v = x.rearrange("(t p) d -> t p d", p=P)
        wg_v = w_gate.rearrange("e (k p) f -> e p k f", p=P)
        wu_v = w_up.rearrange("e (k p) f -> e p k f", p=P)
        wd_v = w_down.rearrange("e (k p) f -> e p k f", p=P)
        NA = len(CHUNKS_A)
        UA = NA * T
        turned = [u for u in range(UA) if CHUNKS_A[u // T][0] != "va"]
        NTURN = len(turned)
        TURN1 = NA1 * T
        LATE = (("row", 2, 0), ("col", 4, 2), ("col", 3, 3), ("row", 5, 1))
        NU = len(SCORED) * NIH

        def cols_of(i):
            return P * (i + 1)

        def tile(t):
            return slice(P * t, P * (t + 1))

        order = []
        for i in range(T + 1):
            for k, then in enumerate(("mix", "norm", "route", None)):
                if i < T:
                    order.append(("heads", (i, 2 * k, 2 * k + 2)))
                if i >= 1 and then:
                    order.append((then, i - 1))
                if i == 1 and then == "norm":
                    order += [("late", 1), ("late", 2)]
            if i < T:
                order.append(("rows", i))
            if i == 0:
                order.append(("late", 0))
            if i == T - 1:
                order.append(("late", 3))
        uses7 = []
        for kind, n in order:
            if kind == "late":
                uses7 += [("late", n, h) for h in range(2)]
            if kind == "mix":
                uses7 += [("mix", n, 0), ("mix", n, 1)]
            if kind == "route":
                uses7.append(("route", n, 0))
        at7 = {use: n for n, use in enumerate(uses7)}

        def late_used(n):
            return at7[("late", n, 1)] + 1

        def groups(i):
            return (i + 4) // 4

        def pt_index(i, h, g):
            return HA * sum(groups(k) for k in range(i)) + h * groups(i) + g

        block = ctx.enter_context(nc.Block())

        @block.sync
        def _(sp):
            for dst, src in ((cst[:, :], const), (cc[:, :], ccol), (bc[:, :, :], b_cols), (gc[:, :, :], g_cols),
                             (posi[:, :], pos)):
                sp.dma_start(dst, src).then_inc(G("ld_const"), 16)
            for t in range(T):
                sp.dma_start(xall[:, t, :], x_v[t]).then_inc(G(f"ld_x{t}"), 16)
            for s, part in enumerate((1, 0)):
                for h in range(2):
                    sp.dma_start(ada_slot[s][:, 4 * h:4 * h + 4], wada_v[:, part, 4 * h:4 * h + 4])\
                        .then_inc(G(f"ld_ada{2 * s + h}"), 16)
            for n, (_, c0, w) in enumerate(CHUNKS_A):
                if n >= 2:
                    sp.wait_ge(G("a_proj"), T * (n - 1))
                sp.dma_start(ring[n % 2][:, :, 0:w], win_v[:, :, c0:c0 + w]).then_inc(G(f"ld_w{n % 2}"), 16)
                if n == NA1 + 1:
                    sp.wait_ge(G("sc_ready"), NU)
                    for k in (2, 3):
                        sp.dma_start(wb[k], win_v[:, :, CHUNKS_B[k][1]:CHUNKS_B[k][1] + 512])\
                            .then_inc(G(f"ld_wb{k}"), 16)
            for k in (0, 1):
                sp.wait_ge(G("a_proj"), UA - T * (1 - k))
                sp.dma_start(wb[k], win_v[:, :, CHUNKS_B[k][1]:CHUNKS_B[k][1] + 512]).then_inc(G(f"ld_wb{k}"), 16)
            for t in range(T):
                if t == T - 1:
                    sp.wait_ge(G("b_proj"), 4 * T)
                    for n in range(2):
                        sp.dma_start(ada_late[n], wada_v[:, LATE[n][1]]).then_inc(G(f"ld_late{n}"), 16)
                    sp.dma_start(wo, wo_v).then_inc(G("ld_wo"), 16)
                sp.wait_ge(G("b_out"), t + 1)
                sp.dma_start(yb_dram[tile(t), :], WB["y"][:, t % 2]).then_inc(G(f"st_yb{t % 2}"), 16)
            sp.wait_ge(G("st_yb0"), 16 * (T // 2))
            sp.wait_ge(G("st_yb1"), 16 * (T // 2))
            sp.wait_ge(G("topk_done"), len(SCORED))
            sp.wait_ge(G("b_qr"), T)
            sp.wait_ge(G("b_kr"), T)
            sp.dma_start(WC["wr"], w_router).then_inc(G("ld_c"), 16)
            sp.dma_start(WC["gt1"], b_gt1).then_inc(G("ld_c"), 16)
            sp.wait_ge(G("c_clear"), 1)
            for q in range(2):
                sp.wait_ge(G(f"st_q{q}"), 16 * (T // 2))
            for i in range(T):
                for n in ((0, 1) if i == 0 else (i + 1,) if i + 1 < T else ()):
                    if n >= 2:
                        sp.wait_ge(G("c_qk"), HA * (n - 1))
                    for h in range(2):
                        sp.dma_start(WC["qBD"][n % 2][64 * h:64 * h + 64, :, h, :],
                                     q_dram[64 * h:64 * h + 64, :, tile(n)]).then_inc(G(f"ld_q{n % 2}"), 16)
                if i >= 1:
                    sp.wait_ge(G("c_ytr"), i)
                sp.dma_start(WC["yb"], yb_dram[tile(i), :]).then_inc(G("ld_yb"), 16)
                if i >= 1:
                    sp.wait_ge(G("c_x1"), i)
                    sp.dma_start(x1_dram[tile(i - 1), :], WC["x"]).then_inc(G("st_x1"), 16)
                    sp.wait_ge(G("c_xn"), i)
                    sp.dma_start(xn_dram[tile(i - 1), :], WC["sq"]).then_inc(G("st_xn"), 16)
                    sp.wait_ge(G("st_x1"), 16 * i)
                sp.dma_start(WC["x"], x_v[i]).then_inc(G("ld_xr"), 16)
            sp.wait_ge(G("c_qk"), HA * T)
            sp.dma_start(gt2, b_gt2).then_inc(G("ld_gt2"), 16)
            sp.wait_ge(G("c_x1"), T)
            sp.dma_start(x1_dram[tile(T - 1), :], WC["x"]).then_inc(G("st_x1"), 16)
            sp.wait_ge(G("c_xn"), T)
            sp.dma_start(xn_dram[tile(T - 1), :], WC["sq"]).then_inc(G("st_xn"), 16)
            sp.wait_ge(G("st_x1"), 16 * T)
            sp.wait_ge(G("r_done"), 1)
            sp.wait_ge(G("b7_ready"), len(uses7))
            pairs = nc.sync.value_load(items[0:1, 63:64], min_val=2, max_val=MAX_ITEMS // 2)

            def weights(j, s, first):
                expert = nc.sync.value_load(items[0:1, bass.ds(2 * j + s, 1)] if not first else
                                            items[0:1, s:s + 1], min_val=0, max_val=NE - 1)
                if not first:
                    sp.wait_ge(G("m_up"), 2 * j + s - 1)
                sp.dma_start(wg[s], wg_v[bass.ds(expert, 1)].squeeze(0)).then_inc(G(f"ld_g{s}"), 16)
                sp.dma_start(wu[s], wu_v[bass.ds(expert, 1)].squeeze(0)).then_inc(G(f"ld_u{s}"), 16)
                if not first:
                    sp.wait_ge(G("m_down"), 2 * j + s - 1)
                sp.dma_start(wd[s], wd_v[bass.ds(expert, 1)].squeeze(0)).then_inc(G(f"ld_d{s}"), 16)

            for s in range(2):
                weights(0, s, True)
            with sp.Fori(1, pairs) as j:
                for s in range(2):
                    weights(j, s, False)
            sp.wait_ge(G("m_end"), 1)
            sp.dma_start(WF["gf"], g_final).then_inc(G("ld_gf"), 16)
            for t in range(T + 1):
                if t < T:
                    if t >= 2:
                        sp.wait_ge(G(f"st_out{t % 2}"), 16 * (t // 2))
                    sp.dma_start(WF["x"][:, t % 2], x1_dram[tile(t), :]).then_inc(G(f"f_x{t % 2}"), 16)
                if t >= 1:
                    sp.wait_ge(G("f_out"), t)
                    sp.dma_start(out[tile(t - 1), :], WF["x"][:, (t - 1) % 2]).then_inc(G(f"st_out{(t - 1) % 2}"), 16)
            for s in range(2):
                sp.wait_ge(G(f"st_out{s}"), 16 * (T // 2))

        @block.gpsimd
        def _(pool):
            own = Own(pool, G("pool_step"))
            tt = nc.gpsimd.tensor_tensor
            own.go(nc.gpsimd.memset(expo[:, :], -0.5))
            own(nc.gpsimd.memset(zero[:, :], 0.0), G("pool_zeros"))
            own(nc.gpsimd.memset(ones[:, :], 1.0), G("pool_ones"))
            own(nc.gpsimd.memset(KV[:, 8192:10240], 0.0), G("pool_zero"))
            pool.wait_ge(G("dve_ms"), 1)
            own(tt(small[:, 8:16], small[:, 0:8], expo[:, :], ALU.pow), G("pool_rstd"))
            for t in range(T):
                pool.wait_ge(G("a_evac"), TURN1 + t + 1)
                pool.dma_start(q_dram[:, :, tile(t)], WA["trq"][:, t % 2].rearrange("p (j s) -> p j s", j=4))\
                    .then_inc(G(f"st_q{t % 2}"), 16)
            pool.wait_ge(G("sc_acc"), NU)
            for q in range(2):
                pool.wait_ge(G(f"st_q{q}"), 16 * (T // 2))
            own(nc.gpsimd.memset(WB["qBD"].rearrange("p j h n -> p (j h n)"), 0.0), G("b_clear"))

            def b_root(t):
                pool.wait_ge(G("b_ms"), t + 1)
                own(tt(small[:, 40:48], small[:, 32:40], expo[:, :], ALU.pow), G("b_rs"))

            for t in range(T):
                q_, k_ = WB["qA"][:, t % 2], WB["kA"][:, t % 2]
                k3 = k_.rearrange("p (h d) -> p h d", h=HB)
                pool.wait_ge(G("b_qsplit"), t + 1)
                own(tt(q_, q_, WB["qB"], ALU.add), G("b_qr"))
                pool.wait_ge(G("b_ksplit"), t + 1)
                own(tt(k_, k_, WB["kB"], ALU.add))
                own(tt(k3, k3, c("kfac").unsqueeze(2).to_broadcast([P, HB, HD]), ALU.mult), G("b_kr"))
                if t >= 1:
                    b_root(t - 1)
            b_root(T - 1)
            pool.wait_ge(G("b_out"), T)
            pool.wait_ge(G("b_y"), T)
            pool.wait_ge(G("topk_done"), len(SCORED))
            for q in range(2):
                pool.wait_ge(G(f"st_yb{q}"), 16 * (T // 2))
            own.go(nc.gpsimd.memset(WC["bias01"], 0.0))
            own(nc.gpsimd.memset(WC["q"], 0.0), G("c_clear"))
            for kind, n in order:
                if kind == "late" and n + 2 < len(LATE):
                    pool.wait_ge(G("b7_ready"), late_used(n))
                    pool.dma_start(ada_late[n % 2], wada_v[:, LATE[n + 2][1]]).then_inc(G(f"ld_late{n + 2}"), 16)
                if kind == "norm":
                    pool.wait_ge(G("c_ms"), n + 1)
                    own(tt(small[:, 49:50], small[:, 48:49], expo[:, 0:1], ALU.pow), G("c_rs"))
            pool.wait_ge(G("r_done"), 1)
            pool.wait_ge(G("st_xn"), 16 * T)
            pairs = nc.gpsimd.value_load(items[0:1, 63:64], min_val=2, max_val=MAX_ITEMS // 2)

            def take_index(column, s):
                nc.gpsimd.tensor_copy(gidx[:, s:s + 1], column).then_inc(G("m_idx"), 1)

            def gather(s):
                nc.gpsimd.indirect_dma_start(
                    out=WM["Xg"][:, s], out_offset=None, in_=xn_dram,
                    in_offset=bass.IndirectOffsetOnAxis(ap=gidx[:, s:s + 1], axis=0)).then_inc(G(f"ld_rows{s}"), 16)

            for i in range(2):
                take_index(tbl[:, i:i + 1], i)
            pool.wait_ge(G("m_idx"), 2)
            gather(0)

            def rows(j, s, first):
                i = 2 * j + s
                pool.wait_ge(G("m_idx"), i + 2)
                if not (first and s == 0):
                    pool.wait_ge(G("m_xtr"), i)
                pool.wait_ge(G(f"ld_rows{s}"), 16 * j + 16)
                take_index(tbl[:, i + 2:i + 3] if first else tbl[:, bass.ds(i + 2, 1)], s)
                gather(1 - s)

            for s in range(2):
                rows(0, s, True)
            with pool.Fori(1, pairs) as j:
                for s in range(2):
                    rows(j, s, False)
            pool.wait_ge(G("m_end"), 1)

            def f_root(t):
                pool.wait_ge(G("f_ms"), t + 1)
                own(tt(small[:, 51:52], small[:, 50:51], expo[:, 0:1], ALU.pow), G("f_rs"))

            for t in range(T):
                if t >= 2:
                    pool.wait_ge(G("f_sum"), t - 1)
                for e, name in enumerate(("y1", "y2")):
                    own(nc.gpsimd.tensor_copy(gidx[:, e:e + 1], srow[:, e, t:t + 1]))
                    nc.gpsimd.indirect_dma_start(
                        out=WF[name][:, t % 2], out_offset=None, in_=y_dram,
                        in_offset=bass.IndirectOffsetOnAxis(ap=gidx[:, e:e + 1], axis=0)).then_inc(
                            G(f"f_y{t % 2}"), 16)
                pool.wait_ge(G(f"f_y{t % 2}"), 32 * (t // 2 + 1))
                if t >= 1:
                    f_root(t - 1)
            f_root(T - 1)

        @block.scalar
        def _(act):
            own = Own(act, G("act_step"))
            A = nc.scalar.activation
            for t in range(T):
                act.wait_ge(G(f"ld_x{t}"), 16)
                own(A(W0["sq"], xall[:, t, :], ACT.Square, accum_out=small[:, 16 + t:17 + t]), G("act_sq"))
            act.wait_ge(G("rope_arg"), 1)

            def flat(a):
                return a.rearrange("p t f -> p (t f)")

            own.go(A(flat(sinT), flat(W0["r"]), ACT.Sin))
            own.go(A(flat(nsinT), flat(W0["r"]), ACT.Sin, scale=-1.0))
            own(A(flat(cosT), flat(W0["c"]), ACT.Sin), G("rope_tab"))
            act.wait_ge(G("pool_zeros"), 1)
            act.wait_ge(G("a_proj"), 2)
            for n in range(4):
                rows = slice(n * MAX_ITEMS // 4 * P, (n + 1) * MAX_ITEMS // 4 * P)
                for h in range(2):
                    act.dma_start(y_dram[rows, 512 * h:512 * h + 512].rearrange("(i p) c -> p i c", p=P),
                                  zero[:, :].unsqueeze(1).to_broadcast([P, MAX_ITEMS // 4, 512]))\
                        .then_inc(G("st_zero"), 16)

            def a_copy(u):
                name, _, w = CHUNKS_A[u // T]
                t = u % T
                act.wait_ge(G("a_proj"), u + 1)
                if name == "va":
                    dst = va[:, t, :]
                    act.wait_ge(G("hT_ready"), T)
                else:
                    m = turned.index(u)
                    if m >= 3:
                        act.wait_ge(G("a_tr"), m - 2)
                    dst = WA["tmp"][:, m % 3, 0:w]
                own.go(A(dst, PS[:, u % 4, 0:w], ACT.Copy), G("a_copied"))

            for u in range(NA1 * T):
                a_copy(u)
            for u in range(NU):
                K = cols_of(FIRST_SCORED + u // NIH)
                b = 2 * (u % 3)
                act.wait_ge(G("sc_ready"), u + 1)
                if u >= 3:
                    act.wait_ge(G("sc_acc"), u - 2)
                own.go(A(WA["R"][:, u % 3, 0:K], PS[:, b:b + 2, :].rearrange("p b c -> p (b c)")[:, 0:K], ACT.Relu),
                       G("sc_relu"))
            for u in range(NA1 * T, UA):
                a_copy(u)

            def b_evacuate(t):
                act.wait_ge(G("b_trq"), t + 1)
                if t == 0:
                    act.wait_ge(G("b_clear"), 1)
                pq = PS[:, 4, :].rearrange("p (j n) -> p j n", j=4)
                own.go(A(WB["qBD"][0:64, :, 0, :], pq[0:64], ACT.Copy))
                own.go(A(WB["qBD"][64:128, :, 1, :], pq[64:128], ACT.Copy), G("b_qbd"))
                act.wait_ge(G("b_trk"), t + 1)
                own.go(A(WB["kT"], PS[:, 5, :].rearrange("p (j n) -> p j n", j=4), ACT.Copy), G("b_kT"))

            act.wait_ge(G("sc_acc"), NU)
            for t in range(T):
                act.wait_ge(G("b_proj"), 4 * t + 3)
                if t >= 2:
                    act.wait_ge(G("b_y"), t - 1)
                    act.wait_ge(G("b_out"), t - 1)
                own.go(A(WB["v"][:, t % 2], PS[:, 2, :], ACT.Copy), G("b_v"))
                act.wait_ge(G("b_proj"), 4 * t + 4)
                own.go(A(WB["g"][:, t % 2], PS[:, 3, :], ACT.Silu), G("b_g"))
                if t >= 1:
                    b_evacuate(t - 1)
            b_evacuate(T - 1)
            act.wait_ge(G("c_clear"), 1)
            for kind, i in order:
                if kind == "heads":
                    i, lo, hi = i
                    K = cols_of(i)
                    for h in range(lo, hi + 1):
                        u = HA * i + h
                        if h < hi:
                            act.wait_ge(G("c_soft"), u + 1)
                            S_ = WC["S"][:, u % 3, 0:K]
                            own.go(A(S_, S_, ACT.Exp, bias=nmax[:, u % 4:u % 4 + 1], scale=-1.0,
                                     accum_out=ssum[:, i % 2, h:h + 1]), G("c_exp"))
                        if h > lo:
                            for g in range(groups(i)):
                                n = pt_index(i, h - 1, g)
                                w = min(512, K - 512 * g)
                                act.wait_ge(G("c_tr"), n + 1)
                                if n >= 2:
                                    act.wait_ge(G("c_pv"), n - 1)
                                own.go(A(WC["PT"][:, n % 2, 0:w], PS[:, 4 + n % 2, 0:w], ACT.Copy), G("c_pt"))
                if kind == "mix":
                    act.wait_ge(G("c_ytr"), i + 1)
                    own.go(A(WC["yT"], PS[:, 4:6, :].rearrange("p b (k n) -> p (b k) n", k=4), ACT.Copy), G("c_yT"))
                if kind == "norm":
                    act.wait_ge(G("c_x1"), i + 1)
                    if i >= 1:
                        act.wait_ge(G("st_xn"), 16 * i)
                        act.wait_ge(G("c_htr"), i)
                    own.go(A(WC["sq"], WC["x"], ACT.Square, accum_out=small[:, 52:53]), G("c_sq"))
            act.wait_ge(G("r_arg"), 1)
            own.go(A(flat(WR["cg"]), flat(WR["cg"]), ACT.Exp))
            own(A(WR["e2x"], WR["e2x"], ACT.Exp), G("r_exp"))
            act.wait_ge(G("r_done"), 1)
            pairs = nc.scalar.value_load(items[0:1, 63:64], min_val=2, max_val=MAX_ITEMS // 2)

            act.wait_ge(G("st_zero"), 16 * 8)

            def item(j, s, first):
                i = 2 * j + s
                act.wait_ge(G("m_gate"), i + 1)
                if not (first and s == 0):
                    act.wait_ge(G("m_h"), i)
                nc.scalar.activation(WM["hs"], PS[:, 2, :], ACT.Silu).then_inc(G("m_silu"), 1)
                act.wait_ge(G("m_down"), i + 1)
                if not first:
                    act.wait_ge(G(f"st_y{s}"), 16 * j)
                nc.scalar.activation(WM["Y"][:, s, 0:512], PS[:, 5, :], ACT.Copy).then_inc(G("m_ya"), 1)
                act.wait_ge(G("m_ya"), i + 1)
                act.wait_ge(G("m_yd"), i + 1)
                rows = bass.ds(i * P, P) if not first else slice(i * P, (i + 1) * P)
                act.dma_start(y_dram[rows, :], WM["Y"][:, s]).then_inc(G(f"st_y{s}"), 16)

            for s in range(2):
                item(0, s, True)
            with act.Fori(1, pairs) as j:
                for s in range(2):
                    item(j, s, False)
            act.wait_ge(G("st_y0"), 16 * pairs)
            act.wait_ge(G("st_y1"), 16 * pairs)
            act.wait_ge(G("m_xT"), 2 * pairs + 1)
            own(A(small[:, 62:63], expo[:, 0:1], ACT.Copy), G("m_end"))
            for t in range(T):
                act.wait_ge(G("f_sum"), t + 1)
                own(A(WF["sq"], WF["x"][:, t % 2], ACT.Square, accum_out=small[:, 53:54]), G("f_sq"))

        @block.vector
        def _(dve):
            own = Own(dve, G("dve_step"))
            V = nc.vector

            def modulate(dst, banks, which):
                for k in range(KD):
                    yield V.tensor_scalar(dst[:, k], PS[:, banks + k // 4, P * (k % 4):P * (k % 4) + P],
                                          mod[:, 2 * which, k:k + 1], mod[:, 2 * which + 1, k:k + 1], ALU.mult,
                                          ALU.add)

            def modulate_all(dst, banks, which, signal):
                for k, ins in enumerate(modulate(dst, banks, which)):
                    own.go(ins, signal if k == KD - 1 else None)

            def own_columns(bank, scratch, at, h, signal):
                s3 = scratch.rearrange("p (k n) -> p k n", k=4)
                own(V.tensor_tensor(s3, PS[:, bank, :].rearrange("p (k n) -> p k n", k=4),
                                    ident.unsqueeze(1).to_broadcast([P, 4, P]), ALU.mult), signal)
                part = mod[:, at, 4 * h:4 * h + 4]
                own(V.tensor_reduce(part, s3, X_AXIS, ALU.add))
                own(V.tensor_tensor(part, part, bc[:, at, 4 * h:4 * h + 4], ALU.add))

            dve.wait_ge(G("ld_const"), 16 * 5)
            own(V.tensor_copy(posf[:, :], posi[:, :]))
            own(V.tensor_tensor(W0["ang"], posf[:, :].unsqueeze(2).to_broadcast([P, T, 40]),
                                c("invf").unsqueeze(1).to_broadcast([P, T, 40]), ALU.mult))
            own(V.tensor_scalar(W0["k"], W0["ang"], 1.0 / TWO_PI, ROUND, ALU.mult, ALU.add))
            own(V.tensor_scalar(W0["k"], W0["k"], ROUND, None, ALU.subtract))
            for part in (PI_HI, PI_MID, PI_LO):
                own(V.scalar_tensor_tensor(W0["ang"], W0["k"], -part, W0["ang"], ALU.mult, ALU.add))
            own(V.tensor_scalar(W0["r"], W0["ang"], PI_IN, -PI_IN, ALU.min, ALU.max))
            own(V.tensor_scalar(W0["c"], W0["ang"], TWO_PI / 4, None, ALU.add))
            own(V.tensor_scalar(W0["k"], W0["c"], TWO_PI / 2, -TWO_PI, ALU.is_gt, ALU.mult))
            own(V.tensor_tensor(W0["c"], W0["c"], W0["k"], ALU.add))
            own(V.tensor_scalar(W0["c"], W0["c"], PI_IN, -PI_IN, ALU.min, ALU.max), G("rope_arg"))
            dve.wait_ge(G("act_sq"), T)
            own(V.tensor_scalar(small[:, 0:8], small[:, 16:24], 1.0 / D, EPS, ALU.mult, ALU.add), G("dve_ms"))
            dve.wait_ge(G("pool_rstd"), 1)
            for t in range(T):
                own.go(V.tensor_scalar(xall[:, t, :], xall[:, t, :], small[:, 8 + t:9 + t], None, ALU.mult),
                       G("xn_ready"))
            for s, at in enumerate((0, 1)):
                dve.wait_ge(G("pe_cols"), s + 1)
                for h in range(2):
                    own_columns(2 * s + h, W0["dg"], at, h, None)
            own(V.scalar_tensor_tensor(mod[:, 0, :], mod[:, 0, :], 1.0, gc[:, 0, :], ALU.add, ALU.mult),
                G("mod_done"))
            for t in range(T):
                dve.wait_ge(G("xt_ready"), t + 1)
                modulate_all(hT[:, :, tile(t)], 4 + 2 * (t % 2), 0, G("hT_ready"))

            def rotate_part(v, t, heads):
                n = 16 * heads
                s1 = WA["s1"][:, 0:n].rearrange("p (h a d) -> p h a d", h=heads, a=2)
                s2 = WA["s2"][:, 0:n].rearrange("p (h a d) -> p h a d", h=heads, a=2)
                wide = [P, heads, 2, 8]
                half = [P, heads, 8]
                own.go(V.tensor_tensor(s1, v, cosT[:, t, 0:8].unsqueeze(1).unsqueeze(1).to_broadcast(wide),
                                       ALU.mult))
                own.go(V.tensor_tensor(s2[:, :, 0], v[:, :, 1], nsinT[:, t, 0:8].unsqueeze(1).to_broadcast(half),
                                       ALU.mult))
                own(V.tensor_tensor(s2[:, :, 1], v[:, :, 0], sinT[:, t, 0:8].unsqueeze(1).to_broadcast(half),
                                    ALU.mult))
                return V.tensor_tensor(v, s1, s2, ALU.add)

            def a_evacuate(m):
                u = turned[m]
                name, t = CHUNKS_A[u // T][0], u % T
                dve.wait_ge(G("a_tr"), m + 1)
                bank = PS[:, 4 + m % 2, :].rearrange("p (j n) -> p j n", j=4)
                if name == "qa":
                    if t >= 2:
                        dve.wait_ge(G(f"st_q{t % 2}"), 16 * (t // 2))
                    ins = V.tensor_copy(WA["trq"][:, t % 2].rearrange("p (j n) -> p j n", j=4), bank)
                elif name == "ka":
                    ins = V.tensor_copy(kaT[:, :, tile(t)], bank)
                elif name in ("qi0", "qi1"):
                    j = 4 * int(name[2])
                    ins = V.tensor_copy(qiT[:, j:j + 4, tile(t)], bank)
                else:
                    own.go(V.tensor_copy(kiBD[0:64, 0, tile(t)], bank[0:64, 0]))
                    ins = V.tensor_copy(kiBD[64:128, 1, tile(t)], bank[64:128, 0])
                own.go(ins, G("a_evac"))

            dve.wait_ge(G("rope_tab"), 1)
            dve.wait_ge(G("pool_zero"), 1)

            def a_rotate(m):
                u = turned[m]
                name, t = CHUNKS_A[u // T][0], u % T
                tmp = WA["tmp"][:, m % 3]
                dve.wait_ge(G("a_copied"), u + 1)
                if name == "kiwi":
                    own.go(V.tensor_scalar(wsc[:, t, :], tmp[:, 64:80], NIH ** -0.5 * HD ** -0.5, None, ALU.mult))
                    own(rotate_part(tmp[:, 0:16].rearrange("p (h a d) -> p h a d", h=1, a=2), t, 1))
                    own(V.tensor_copy(tmp[:, 64:128], tmp[:, 0:64]), G("a_rot"))
                else:
                    v = tmp.rearrange("p (h c) -> p h c", h=8)[:, :, 0:16].rearrange("p h (a d) -> p h a d", a=2)
                    own(rotate_part(v, t, 8), G("a_rot"))

            for m in range(TURN1):
                a_rotate(m)
                if m >= 1:
                    a_evacuate(m - 1)
            a_evacuate(TURN1 - 1)
            own.wait()
            for u in range(NU):
                i, h = FIRST_SCORED + u // NIH, u % NIH
                K = cols_of(i)
                acc = ACC[:, ACC_OFF[i]:ACC_OFF[i] + K]
                R = WA["R"][:, u % 3, 0:K]
                dve.wait_ge(G("sc_relu"), u + 1)
                if h == 0:
                    own(V.tensor_scalar(acc, R, wsc[:, i, h:h + 1], None, ALU.mult), G("sc_acc"))
                else:
                    own(V.scalar_tensor_tensor(acc, R, wsc[:, i, h:h + 1], acc, ALU.mult, ALU.add), G("sc_acc"))
                if h == NIH - 1:
                    own(V.scalar_tensor_tensor(acc[:, K - 64:K], c("unseen"), NEG_SCORE, acc[:, K - 64:K], ALU.mult,
                                               ALU.add))

            def top_k():
                for i in SCORED:
                    K = cols_of(i)
                    acc = ACC[:, ACC_OFF[i]:ACC_OFF[i] + K]
                    own(V.tensor_copy(Wk[:, 0:K], acc))
                    for _ in range(TOPK // 8):
                        own(V.max(m8, Wk[:, 0:K]))
                        own(V.match_replace(Wk[:, 0:K], m8, Wk[:, 0:K], TAKEN))
                        yield 2 * K / 960 + 0.2
                    own(V.tensor_tensor(acc, acc, Wk[:, 0:K], ALU.is_equal))
                    own(V.tensor_scalar(acc, acc, NEG_LOGIT, None, ALU.mult), G("topk_done"))
                    yield K / 640 + 0.2

            pieces = top_k()

            def spend(us):
                while us > 0:
                    took = next(pieces, None)
                    if took is None:
                        return
                    us -= took

            for m in range(TURN1, NTURN):
                a_rotate(m)
                spend(4.6)
                if m > TURN1:
                    a_evacuate(m - 1)
            a_evacuate(NTURN - 1)
            own.wait()
            spend(7.0 * T)

            def b_rotate(t):
                for bank, a, b, signal in ((0, WB["qA"][:, t % 2], WB["qB"], "b_qsplit"),
                                           (1, WB["kA"][:, t % 2], WB["kB"], "b_ksplit")):
                    dve.wait_ge(G("b_proj"), 4 * t + bank + 1)
                    if t >= 1:
                        dve.wait_ge(G("b_qr" if bank == 0 else "b_kr"), t)
                    if t >= 2:
                        dve.wait_ge(G("b_y"), t - 1)
                    src = PS[:, bank, :].rearrange("p (h a d) -> p h a d", h=HB, a=2)
                    a4 = a.rearrange("p (h a d) -> p h a d", h=HB, a=2)
                    b4 = b.rearrange("p (h a d) -> p h a d", h=HB, a=2)
                    half = [P, HB, 32]
                    own.go(V.tensor_tensor(a4, src, cosT[:, t, 8:40].unsqueeze(1).unsqueeze(1)
                                           .to_broadcast([P, HB, 2, 32]), ALU.mult))
                    own.go(V.tensor_tensor(b4[:, :, 0], src[:, :, 1],
                                           nsinT[:, t, 8:40].unsqueeze(1).to_broadcast(half), ALU.mult))
                    own.go(V.tensor_tensor(b4[:, :, 1], src[:, :, 0],
                                           sinT[:, t, 8:40].unsqueeze(1).to_broadcast(half), ALU.mult), G(signal))

            def b_retain(t):
                dve.wait_ge(G("b_s"), t + 1)
                if t >= 1:
                    dve.wait_ge(G("b_y"), t)
                for half in range(2):
                    own.go(V.tensor_tensor(WB["S"][:, 4 * half:4 * half + 4],
                                           PS[:, 6 + half, :].rearrange("p (h n) -> p h n", h=4),
                                           c("causal").unsqueeze(1).to_broadcast([P, 4, P]), ALU.mult),
                           G("b_sm") if half else None)
                spend(B_SPEND[1])
                dve.wait_ge(G("b_y"), t + 1)
                if t >= 2:
                    dve.wait_ge(G(f"st_yb{t % 2}"), 16 * (t // 2))
                y = WB["y"][:, t % 2]
                y3 = y.rearrange("p (h d) -> p h d", h=HB)
                sq3 = WB["sq"].rearrange("p (h d) -> p h d", h=HB)
                per = [P, HB, HD]
                own(V.tensor_tensor(y3, PS[:, 4, :].rearrange("p (h d) -> p h d", h=HB),
                                    c("xi").unsqueeze(2).to_broadcast(per), ALU.mult), G("b_yread"))
                if t < T - 1:
                    kv = PS[:, 5, :].rearrange("p (j e) -> p j e", j=4)
                    dve.wait_ge(G("b_kv"), t + 1)
                    if t >= 1:
                        own(V.tensor_tensor(WB["st"], WB["st"], kv, ALU.add))
                        src = WB["st"]
                    else:
                        src = kv
                    own(V.tensor_tensor(WB["st"], src, c("carry").rearrange("p (j e) -> p j e", j=4), ALU.mult),
                        G("b_state"))
                own(V.tensor_reduce(small[:, 24:32], y3, X_AXIS, ALU.add))
                own(V.tensor_scalar(small[:, 24:32], small[:, 24:32], 1.0 / HD, None, ALU.mult))
                own(V.tensor_tensor(y3, y3, small[:, 24:32].unsqueeze(2).to_broadcast(per), ALU.subtract))
                own(V.tensor_tensor(sq3, y3, y3, ALU.mult))
                own(V.tensor_reduce(small[:, 24:32], sq3, X_AXIS, ALU.add))
                own(V.tensor_scalar(small[:, 32:40], small[:, 24:32], 1.0 / HD, EPS, ALU.mult, ALU.add), G("b_ms"))
                dve.wait_ge(G("b_g"), t + 1)
                own(V.tensor_tensor(y, y, WB["g"][:, t % 2], ALU.mult))
                dve.wait_ge(G("b_rs"), t + 1)
                own(V.tensor_tensor(y3, y3, small[:, 40:48].unsqueeze(2).to_broadcast(per), ALU.mult), G("b_out"))

            for q in range(2):
                dve.wait_ge(G(f"st_q{q}"), 16 * (T // 2))
            for t in range(T):
                b_rotate(t)
                spend(B_SPEND[0])
                if t >= 1:
                    b_retain(t - 1)
                    spend(B_SPEND[2])
            b_retain(T - 1)
            for _ in pieces:
                pass
            dve.wait_ge(G("c_clear"), 1)
            dve.wait_ge(G("ld_c"), 16 * 2)
            own(V.tensor_scalar(WC["bias01"][:, 192:256], c("unseen"), NEG_LOGIT, None, ALU.mult))

            def negated_logits(u):
                i = u // HA
                K = cols_of(i)
                bias = WC["bias01"][:, 256 - K:256] if i < FIRST_SCORED else ACC[:, ACC_OFF[i]:ACC_OFF[i] + K]
                b = 2 * (u % 2)
                dve.wait_ge(G("c_qk"), u + 1)
                if u >= 3:
                    pi, ph = divmod(u - 3, HA)
                    dve.wait_ge(G("c_tr"), pt_index(pi, ph, groups(pi) - 1) + 1)
                own.go(V.tensor_tensor_reduce(
                    out=WC["S"][:, u % 3, 0:K], in0=PS[:, b:b + 2, :].rearrange("p b c -> p (b c)")[:, 0:K],
                    in1=bias, scale=-HD ** -0.5, scalar=3.0e38, op0=ALU.add, op1=ALU.min,
                    accum_out=nmax[:, u % 4:u % 4 + 1]), G("c_soft"))

            negated_logits(0)
            negated_logits(1)
            for kind, i in order:
                if kind == "heads":
                    i, lo, hi = i
                    for u in range(HA * i + lo + 2, min(HA * i + hi + 2, HA * T)):
                        negated_logits(u)
                if kind == "late":
                    shape, part, at = LATE[i]
                    for h in range(2):
                        n7 = at7[("late", i, h)]
                        dve.wait_ge(G("b7_ready"), n7 + 1)
                        if shape == "row":
                            if at == 1:
                                dve.wait_ge(G("ld_gt2"), 16)
                            dst = (WC["gt1"] if at == 0 else gt2)[:, 512 * h:512 * h + 512]
                            own(V.tensor_tensor(dst, PS[:, 7, :], dst, ALU.add), G("b7_free"))
                        else:
                            own_columns(7, WC["y"], at, h, G("b7_free"))
                            if at == 2 and h == 1:
                                own(V.scalar_tensor_tensor(mod[:, 2, :], mod[:, 2, :], 1.0, gc[:, 1, :], ALU.add,
                                                           ALU.mult))
                if kind == "rows":
                    dve.wait_ge(G("c_exp"), HA * (i + 1))
                    own(V.reciprocal(ssum[:, i % 2, :], ssum[:, i % 2, :]))
                    dve.wait_ge(G("c_pv"), pt_index(i, HA - 1, groups(i) - 1) + 1)
                    if i >= 1:
                        dve.wait_ge(G("c_ytr"), i)
                    own(V.tensor_tensor(WC["y"].rearrange("p (h d) -> p h d", h=HA),
                                        PS[:, 6, :].rearrange("p (h d) -> p h d", h=HA),
                                        ssum[:, i % 2, :].unsqueeze(2).to_broadcast([P, HA, HD]), ALU.mult), G("c_y"))
                if kind == "mix":
                    dve.wait_ge(G("ld_xr"), 16 * (i + 1))
                    if i >= 1:
                        dve.wait_ge(G("c_htr"), i)
                        dve.wait_ge(G("st_xn"), 16 * i)
                    for h in range(2):
                        n7 = at7[("mix", i, h)]
                        part = slice(512 * h, 512 * h + 512)
                        dve.wait_ge(G("b7_ready"), n7 + 1)
                        own(V.tensor_tensor(WC["sq"][:, part], PS[:, 7, :], WC["gt1"][:, part], ALU.mult),
                            G("b7_free"))
                        own(V.tensor_tensor(WC["x"][:, part], WC["x"][:, part], WC["sq"][:, part], ALU.add),
                            G("c_x1") if h else None)
                if kind == "norm":
                    dve.wait_ge(G("c_sq"), i + 1)
                    own(V.tensor_scalar(small[:, 48:49], small[:, 52:53], 1.0 / D, EPS, ALU.mult, ALU.add),
                        G("c_ms"))
                    dve.wait_ge(G("c_rs"), i + 1)
                    own(V.tensor_scalar(WC["sq"], WC["x"], small[:, 49:50], None, ALU.mult), G("c_xn"))
                if kind == "route":
                    dve.wait_ge(G("c_htr"), i + 1)
                    modulate_all(WC["h2T"], 4, 1, G("c_h2"))
                    dve.wait_ge(G("b7_ready"), at7[("route", i, 0)] + 1)
                    own(V.tensor_copy(L[:, i, :], PS[:, 7, 0:36]), G("b7_free"))
            dve.wait_ge(G("st_x1"), 16 * T)
            dve.wait_ge(G("st_xn"), 16 * T)
            q8 = [P, T, 8]
            desc = c("desc")

            def largest(values, n, top, first, scratch):
                own(V.tensor_reduce(top, values, X_AXIS, ALU.max))
                own(V.tensor_tensor(scratch, values, top.unsqueeze(2).to_broadcast([P, T, n]), ALU.is_equal))
                own(V.tensor_tensor(scratch, scratch, desc[:, 8 - n:8].unsqueeze(1).to_broadcast([P, T, n]),
                                    ALU.mult))
                own(V.tensor_reduce(WR["m"], scratch, X_AXIS, ALU.max))
                own(V.tensor_tensor(first, scratch, WR["m"].unsqueeze(2).to_broadcast([P, T, n]), ALU.is_equal))

            Lg = L[:, :, 0:NG]
            largest(Lg, NG, WR["gm"], WR["G"], WR["cg"])
            own(V.tensor_tensor(WR["cg"], Lg, WR["gm"].unsqueeze(2).to_broadcast([P, T, NG]), ALU.subtract))
            own(V.tensor_tensor(WR["tmp"].rearrange("p t (g e) -> p t g e", g=NG),
                                L[:, :, NG:36].rearrange("p t (g e) -> p t g e", g=NG),
                                WR["G"].unsqueeze(3).to_broadcast([P, T, NG, EPG]), ALU.mult))
            own(V.tensor_reduce(WR["f"], WR["tmp"].rearrange("p t (g e) -> p t e g", g=NG), X_AXIS, ALU.add))
            largest(WR["f"], 8, WR["t1"], WR["o1"], WR["ca"])
            own(V.scalar_tensor_tensor(WR["f2"], WR["o1"], TAKEN, WR["f"], ALU.mult, ALU.add))
            largest(WR["f2"], 8, WR["t2"], WR["o2"], WR["ca"])
            own(V.tensor_tensor(WR["e2x"], WR["t2"], WR["t1"], ALU.subtract), G("r_arg"))
            dve.wait_ge(G("r_exp"), 1)
            own(V.tensor_reduce(WR["gm"], WR["cg"], X_AXIS, ALU.add))
            own(V.tensor_scalar(WR["t1"], WR["e2x"], 1.0, None, ALU.add))
            own(V.tensor_tensor(WR["t1"], WR["t1"], WR["gm"], ALU.mult))
            own(V.reciprocal(sw[:, 0, :], WR["t1"]))
            own(V.tensor_tensor(sw[:, 1, :], sw[:, 0, :], WR["e2x"], ALU.mult))
            for e, o in (("e1", "o1"), ("e2", "o2")):
                own(V.tensor_tensor(WR[e].rearrange("p t (g e) -> p t g e", g=NG),
                                    WR["G"].unsqueeze(3).to_broadcast([P, T, NG, EPG]),
                                    WR[o].unsqueeze(2).to_broadcast([P, T, NG, EPG]), ALU.mult))
            own(V.tensor_tensor(WR["A"], WR["e1"], WR["e2"], ALU.add))
            own(V.memset(WR["pre"][:, 0], 0.0))
            for t in range(1, T):
                own(V.tensor_tensor(WR["pre"][:, t], WR["pre"][:, t - 1], WR["A"][:, t - 1], ALU.add))
            own(V.tensor_tensor(WR["cnt"], WR["pre"][:, T - 1], WR["A"][:, T - 1], ALU.add), G("r_dve"))
            dve.wait_ge(G("r_pe"), 1)
            rank = PS[:, 0, 0:256].rearrange("p (t e) -> p t e", t=T)
            own(V.tensor_copy(WR["cnt"], PS[:, 1, 0:NE]))
            ends, nb = WR["ends"], WR["nb"]
            own(V.tensor_scalar(nb, WR["cnt"], 0.0, None, ALU.is_gt))
            for k in range(1, T):
                own(V.scalar_tensor_tensor(nb, WR["cnt"], float(P * k), nb, ALU.is_gt, ALU.add))
            own(V.tensor_copy(ends[:, 0], nb))
            for n, step in enumerate((1, 2, 4, 8, 16)):
                src, dst = ends[:, n % 2], ends[:, (n + 1) % 2]
                own(V.tensor_copy(dst[:, 0:step], src[:, 0:step]))
                own(V.tensor_tensor(dst[:, step:NE], src[:, step:NE], src[:, 0:NE - step], ALU.add))
            end = ends[:, 1]
            own(V.tensor_tensor(WR["start"], end, nb, ALU.subtract))
            own(V.scalar_tensor_tensor(WR["V"], WR["start"].unsqueeze(1).to_broadcast([P, T, NE]), float(P), rank,
                                       ALU.mult, ALU.add))
            for e, name in enumerate(("e1", "e2")):
                own(V.tensor_tensor(WR["tmp"], WR[name], WR["V"], ALU.mult))
                own(V.tensor_reduce(WR["row"][:, e], WR["tmp"], X_AXIS, ALU.add))
                own(V.tensor_copy(srow[:, e, :], WR["row"][:, e]))
            row16 = WR["row"].rearrange("p e t -> p (e t)")
            q16 = WR["q"].rearrange("p e t -> p (e t)")
            r16 = WR["r"].rearrange("p e t -> p (e t)")
            it3 = WR["it"][:, 0:768].rearrange("p (r k) -> p r k", r=16)
            own(V.tensor_scalar(WR["h48"], c("iota")[:, 1:49], float(P), None, ALU.mult))
            own(V.tensor_tensor(it3, row16.unsqueeze(2).to_broadcast([P, 16, 48]),
                                WR["h48"].unsqueeze(1).to_broadcast([P, 16, 48]), ALU.is_ge))
            own(V.tensor_reduce(q16, it3, X_AXIS, ALU.add))
            own(V.scalar_tensor_tensor(r16, q16, -float(P), row16, ALU.mult, ALU.add))
            for n in range(2 * T):
                e, t = divmod(n, T)
                if n >= 2:
                    dve.wait_ge(G("r_acc"), n - 1)
                own.go(V.tensor_scalar(WR["ohp"][:, n % 2], c("iota"), WR["r"][:, e, t:t + 1], None, ALU.is_equal))
                own.go(V.tensor_scalar(WR["ohi"][:, n % 2], c("iota")[:, 0:64], WR["q"][:, e, t:t + 1],
                                       c("token")[:, t:t + 1], ALU.is_equal, ALU.mult), G("r_oh"))
            own.wait()
            it2 = WR["it"][0:1, 0:MAX_ITEMS * NE].rearrange("p (i e) -> p i e", i=MAX_ITEMS)
            own(V.tensor_tensor(it2, end[0:1].unsqueeze(1).to_broadcast([1, MAX_ITEMS, NE]),
                                c("iota")[0:1, 0:MAX_ITEMS].unsqueeze(2).to_broadcast([1, MAX_ITEMS, NE]),
                                ALU.is_le))
            own(V.tensor_reduce(WR["ef"][0:1, 0:MAX_ITEMS], it2, X_AXIS, ALU.add))
            own(V.tensor_scalar(WR["ef"][0:1, 0:MAX_ITEMS], WR["ef"][0:1, 0:MAX_ITEMS], float(NE - 1), None,
                                ALU.min))
            own(V.tensor_scalar(WR["h"][0:1, 0:MAX_ITEMS // 2], c("even")[0:1, :], end[0:1, NE - 1:NE], None,
                                ALU.is_lt))
            own(V.tensor_reduce(WR["h"][0:1, 32:33], WR["h"][0:1, 0:MAX_ITEMS // 2], X_AXIS, ALU.add))
            own(V.tensor_copy(items[0:1, 0:MAX_ITEMS], WR["ef"][0:1, 0:MAX_ITEMS]))
            own(V.tensor_copy(items[0:1, 63:64], WR["h"][0:1, 32:33]))
            dve.wait_ge(G("r_acc"), 2 * T)
            own(V.tensor_copy(tbl[:, :], PS[:, 2, 0:TBL]), G("r_done"))

            pairs = nc.vector.value_load(items[0:1, 63:64], min_val=2, max_val=MAX_ITEMS // 2)

            def turned_rows(s, count):
                dve.wait_ge(G("m_xtr"), count)
                for k, ins in enumerate(modulate(WM["xT"][:, s], 0, 1)):
                    ins.then_inc(G("m_xT") if k == KD - 1 else G("m_part"), 1)

            def item(j, s, first):
                i = 2 * j + s
                dve.wait_ge(G("m_silu"), i + 1)
                dve.wait_ge(G("m_up"), i + 1)
                V.tensor_tensor(WM["h"][:, s], WM["hs"], PS[:, 3, :], ALU.mult).then_inc(G("m_h"), 1)
                turned_rows(1 - s, i + 2)
                dve.wait_ge(G("m_htr"), i + 1)
                V.tensor_copy(WM["hT"][:, s], PS[:, 4, :].rearrange("p (k n) -> p k n", k=KF)).then_inc(G("m_hT"), 1)
                dve.wait_ge(G("m_down"), i + 1)
                if not first:
                    dve.wait_ge(G(f"st_y{s}"), 16 * j)
                V.tensor_copy(WM["Y"][:, s, 512:1024], PS[:, 6, :]).then_inc(G("m_yd"), 1)

            turned_rows(0, 1)
            for s in range(2):
                item(0, s, True)
            with dve.Fori(1, pairs) as j:
                for s in range(2):
                    item(j, s, False)
            dve.wait_ge(G("m_end"), 1)
            dve.wait_ge(G("ld_gf"), 16)
            for t in range(T):
                s = t % 2
                xf, y1, y2 = WF["x"][:, s], WF["y1"][:, s], WF["y2"][:, s]
                dve.wait_ge(G(f"f_y{s}"), 32 * (t // 2 + 1))
                own(V.tensor_scalar(y1, y1, sw[:, 0, t:t + 1], None, ALU.mult))
                own(V.scalar_tensor_tensor(y1, y2, sw[:, 1, t:t + 1], y1, ALU.mult, ALU.add))
                own(V.tensor_tensor(y1, y1, gt2, ALU.mult))
                dve.wait_ge(G(f"f_x{s}"), 16 * (t // 2 + 1))
                own(V.tensor_tensor(xf, xf, y1, ALU.add), G("f_sum"))
                dve.wait_ge(G("f_sq"), t + 1)
                own(V.tensor_scalar(small[:, 50:51], small[:, 53:54], 1.0 / D, EPS, ALU.mult, ALU.add), G("f_ms"))
                dve.wait_ge(G("f_rs"), t + 1)
                own(V.scalar_tensor_tensor(xf, xf, small[:, 51:52], WF["gf"], ALU.mult, ALU.mult), G("f_out"))

        @block.tensor
        def _(pe):
            mm, tr = nc.tensor.matmul, nc.tensor.transpose

            def matvec(bank, weights, h, ds_):
                for d in ds_:
                    last = mm(PS[:, bank, :], cc[:, d:d + 1].to_broadcast([P, P]), weights[:, d, 512 * h:512 * h + 512],
                              start=(d == 0), stop=(d == KD - 1))
                return last

            def turn_rows(rows, bank):
                for k in range(KD):
                    last = tr(PS[:, bank + k // 4, P * (k % 4):P * (k % 4) + P], rows[:, P * k:P * k + P], ident)
                return last

            pe.wait_ge(G("ld_const"), 16 * 5)
            pe.wait_ge(G("pool_ones"), 1)
            for s in range(2):
                for d4 in range(2):
                    pe.wait_ge(G(f"ld_ada{2 * s + d4}"), 16)
                    for h in range(2):
                        last = matvec(2 * s + h, ada_slot[s], h, range(4 * d4, 4 * d4 + 4))
                last.then_inc(G("pe_cols"), 1)
            pe.wait_ge(G("mod_done"), 1)
            for t in range(T):
                pe.wait_ge(G("xn_ready"), t + 1)
                if t >= 2:
                    pe.wait_ge(G("hT_ready"), t - 1)
                turn_rows(xall[:, t, :], 4 + 2 * (t % 2)).then_inc(G("xt_ready"), 1)

            def a_turn(m):
                u = turned[m]
                pe.wait_ge(G("a_rot"), m + 1)
                if m >= 2:
                    pe.wait_ge(G("a_evac"), m - 1)
                n = 1 if CHUNKS_A[u // T][0] == "kiwi" else 4
                for k in range(n):
                    last = tr(PS[:, 4 + m % 2, P * k:P * k + P], WA["tmp"][:, m % 3, P * k:P * k + P], ident)
                last.then_inc(G("a_tr"), 1)

            def a_project(chunks):
                m = turned.index(chunks[0] * T)
                m0 = m
                for n in chunks:
                    name, _, w = CHUNKS_A[n]
                    pe.wait_ge(G(f"ld_w{n % 2}"), 16 * (n // 2 + 1))
                    for t in range(T):
                        u = n * T + t
                        if n == 0:
                            pe.wait_ge(G("hT_ready"), t + 1 if t > 1 else T)
                        if u >= 4:
                            pe.wait_ge(G("a_copied"), u - 3)
                        for k in range(KD):
                            last = mm(PS[:, u % 4, 0:w], hT[:, k, tile(t)], ring[n % 2][:, k, 0:w], start=(k == 0),
                                      stop=(k == KD - 1))
                        last.then_inc(G("a_proj"), 1)
                        if name != "va":
                            if m > m0:
                                a_turn(m - 1)
                            m += 1
                        elif t == 0:
                            a_turn(m - 1)
                if name != "va":
                    a_turn(m - 1)

            a_project(range(NA1))
            pe.wait_ge(G("a_copied"), NA1 * T)
            pe.wait_ge(G("a_evac"), TURN1)
            for u in range(NU):
                i, h = FIRST_SCORED + u // NIH, u % NIH
                K = cols_of(i)
                if u >= 3:
                    pe.wait_ge(G("sc_relu"), u - 2)
                for b in range((K + 511) // 512):
                    w = min(512, K - 512 * b)
                    last = mm(PS[:, 2 * (u % 3) + b, 0:w], qiT[:, h // 2, tile(i)], kiBD[:, h % 2, 512 * b:512 * b + w],
                              start=True, stop=True)
                last.then_inc(G("sc_ready"), 1)
            pe.wait_ge(G("sc_relu"), NU)
            a_project(range(NA1, NA))
            pe.wait_ge(G("a_copied"), UA)
            pe.wait_ge(G("a_evac"), NTURN)

            def b_retain(t):
                q_, k_, v_ = WB["qA"][:, t % 2], WB["kA"][:, t % 2], WB["v"][:, t % 2]
                pe.wait_ge(G("b_qr"), t + 1)
                if t >= 1:
                    pe.wait_ge(G("b_yread"), t)
                for j in range(4):
                    last = tr(PS[:, 4, P * j:P * j + P], q_[:, P * j:P * j + P], ident)
                last.then_inc(G("b_trq"), 1)
                pe.wait_ge(G("b_kr"), t + 1)
                if t >= 1:
                    pe.wait_ge(G("b_state"), t)
                for j in range(4):
                    last = tr(PS[:, 5, P * j:P * j + P], k_[:, P * j:P * j + P], ident)
                last.then_inc(G("b_trk"), 1)
                pe.wait_ge(G("b_qbd"), t + 1)
                pe.wait_ge(G("b_kT"), t + 1)
                if t >= 1:
                    pe.wait_ge(G("b_sm"), t)
                for j in range(4):
                    last = mm(PS[:, 6 + j // 2, 256 * (j % 2):256 * (j % 2) + 256], WB["kT"][:, j, :],
                              WB["qBD"][:, j].rearrange("p h n -> p (h n)"), start=True, stop=True)
                last.then_inc(G("b_s"), 1)
                pe.wait_ge(G("b_v"), t + 1)
                if t < T - 1:
                    for j in range(4):
                        last = mm(PS[:, 5, P * j:P * j + P], k_[:, P * j:P * j + P], v_[:, P * j:P * j + P],
                                  start=True, stop=True)
                    last.then_inc(G("b_kv"), 1)
                pe.wait_ge(G("b_sm"), t + 1)
                for h in range(HB):
                    o = PS[:, 4, HD * h:HD * h + HD]
                    if t >= 1:
                        mm(o, WB["qBD"][:, h // 2, h % 2, :], WB["st"][:, h // 2, HD * (h % 2):HD * (h % 2) + HD],
                           start=True, stop=False)
                    last = mm(o, WB["S"][:, h, :], v_[:, HD * h:HD * h + HD], start=(t == 0), stop=True)
                last.then_inc(G("b_y"), 1)

            for t in range(T):
                for k in range(4):
                    if t == 0:
                        pe.wait_ge(G(f"ld_wb{k}"), 16)
                    else:
                        pe.wait_ge(G(("b_qsplit", "b_ksplit", "b_v", "b_g")[k]), t)
                    for d in range(KD):
                        last = mm(PS[:, k, :], hT[:, d, tile(t)], wb[k][:, d, :], start=(d == 0), stop=(d == KD - 1))
                    last.then_inc(G("b_proj"), 1)
                if t >= 1:
                    b_retain(t - 1)
            b_retain(T - 1)
            for name in ("b_qsplit", "b_ksplit", "b_v", "b_g", "b_yread", "b_sm"):
                pe.wait_ge(G(name), T)
            pe.wait_ge(G("b_state"), T - 1)

            def bank7(use):
                if at7[use] >= 1:
                    pe.wait_ge(G("b7_free"), at7[use])

            def query_keys(u):
                i, h = divmod(u, HA)
                K = cols_of(i)
                if h == 0:
                    pe.wait_ge(G(f"ld_q{i % 2}"), 32 * (i // 2 + 1))
                if u >= 2:
                    pe.wait_ge(G("c_soft"), u - 1)
                for b in range((K + 511) // 512):
                    w = min(512, K - 512 * b)
                    last = mm(PS[:, 2 * (u % 2) + b, 0:w], WC["qBD"][i % 2][:, h // 2, h % 2, :],
                              kaT[:, h // 2, 512 * b:512 * b + w], start=True, stop=True)
                last.then_inc(G("c_qk"), 1)

            def values(i, h, g):
                n = pt_index(i, h, g)
                pe.wait_ge(G("c_pt"), n + 1)
                if h == 0 and g == 0 and i >= 1:
                    pe.wait_ge(G("c_y"), i)
                for b in range(4 * g, min(4 * g + 4, i + 1)):
                    last = mm(PS[:, 6, HD * h:HD * h + HD], WC["PT"][:, n % 2, P * (b % 4):P * (b % 4) + P],
                              va[:, b, HD * h:HD * h + HD], start=(b == 0), stop=(b == i))
                last.then_inc(G("c_pv"), 1)

            for kind, i in order:
                if kind == "heads":
                    i, lo, hi = i
                    if i == 0 and lo == 0:
                        query_keys(0)
                        query_keys(1)
                    todo = None
                    for h in range(lo, hi):
                        if HA * i + h + 2 < HA * T:
                            query_keys(HA * i + h + 2)
                        for g in range(groups(i)):
                            n = pt_index(i, h, g)
                            pe.wait_ge(G("c_exp"), HA * i + h + 1)
                            if n >= 2:
                                pe.wait_ge(G("c_pt"), n - 1)
                            for b in range(4 * g, min(4 * g + 4, i + 1)):
                                last = tr(PS[:, 4 + n % 2, P * (b % 4):P * (b % 4) + P],
                                          WC["S"][:, (HA * i + h) % 3, P * b:P * b + P], ident)
                            last.then_inc(G("c_tr"), 1)
                            if todo:
                                values(*todo)
                            todo = (i, h, g)
                    values(*todo)
                if kind == "late":
                    shape, _, at = LATE[i]
                    pe.wait_ge(G(f"ld_late{i}"), 16)
                    w_ = ada_late[i % 2]
                    for h in range(2):
                        bank7(("late", i, h))
                        matvec(7, w_, h, range(KD)).then_inc(G("b7_ready"), 1)
                if kind == "mix":
                    pe.wait_ge(G("c_y"), i + 1)
                    pe.wait_ge(G("ld_yb"), 16 * (i + 1))
                    for k in range(8):
                        src = WC["y"] if k < 4 else WC["yb"]
                        last = tr(PS[:, 4 + k // 4, P * (k % 4):P * (k % 4) + P],
                                  src[:, P * (k % 4):P * (k % 4) + P], ident)
                    last.then_inc(G("c_ytr"), 1)
                    pe.wait_ge(G("c_yT"), i + 1)
                    pe.wait_ge(G("ld_wo"), 16)
                    for h in range(2):
                        bank7(("mix", i, h))
                        for k in range(KD):
                            last = mm(PS[:, 7, :], WC["yT"][:, k, :], wo[:, k, 512 * h:512 * h + 512], start=(k == 0),
                                      stop=(k == KD - 1))
                        last.then_inc(G("b7_ready"), 1)
                if kind == "route":
                    pe.wait_ge(G("c_xn"), i + 1)
                    turn_rows(WC["sq"], 4).then_inc(G("c_htr"), 1)
                    pe.wait_ge(G("c_h2"), i + 1)
                    bank7(("route", i, 0))
                    pe.wait_ge(G("ld_c"), 16 * 2)
                    for k in range(KD):
                        last = mm(PS[:, 7, 0:36], WC["h2T"][:, k, :], WC["wr"][:, 36 * k:36 * k + 36],
                                  start=(k == 0), stop=(k == KD - 1))
                    last.then_inc(G("b7_ready"), 1)
            pe.wait_ge(G("r_dve"), 1)
            rank = PS[:, 0, 0:256]
            mm(rank, c("before"), WR["A"].rearrange("p t e -> p (t e)"), start=True, stop=False)
            mm(rank, ones[:, :], WR["pre"].rearrange("p t e -> p (t e)"), start=False, stop=True)
            mm(PS[:, 1, 0:NE], ones[:, :], WR["cnt"], start=True, stop=True).then_inc(G("r_pe"), 1)
            for n in range(2 * T):
                pe.wait_ge(G("r_oh"), n + 1)
                mm(PS[:, 2, 0:64], WR["ohp"][:, n % 2], WR["ohi"][:, n % 2], start=(n == 0),
                   stop=(n == 2 * T - 1)).then_inc(G("r_acc"), 1)
            pe.wait_ge(G("r_done"), 1)
            pairs = nc.tensor.value_load(items[0:1, 63:64], min_val=2, max_val=MAX_ITEMS // 2)
            pe.wait_ge(G("ld_rows0"), 16)
            turn_rows(WM["Xg"][:, 0], 0).then_inc(G("m_xtr"), 1)

            def item(j, s, first):
                i = 2 * j + s
                any_before = not (first and s == 0)
                pe.wait_ge(G("m_xT"), i + 1)
                pe.wait_ge(G(f"ld_g{s}"), 16 * j + 16)
                if any_before:
                    pe.wait_ge(G("m_silu"), i)
                for k in range(KD):
                    last = mm(PS[:, 2, :], WM["xT"][:, s, k, :], wg[s][:, k, :], start=(k == 0), stop=(k == KD - 1))
                last.then_inc(G("m_gate"), 1)
                pe.wait_ge(G(f"ld_u{s}"), 16 * j + 16)
                if any_before:
                    pe.wait_ge(G("m_h"), i)
                for k in range(KD):
                    last = mm(PS[:, 3, :], WM["xT"][:, s, k, :], wu[s][:, k, :], start=(k == 0), stop=(k == KD - 1))
                last.then_inc(G("m_up"), 1)
                pe.wait_ge(G(f"ld_rows{1 - s}"), 16 * j + 16 + 16 * s)
                turn_rows(WM["Xg"][:, 1 - s], 0).then_inc(G("m_xtr"), 1)
                pe.wait_ge(G("m_h"), i + 1)
                if any_before:
                    pe.wait_ge(G("m_hT"), i)
                for k in range(KF):
                    last = tr(PS[:, 4, P * k:P * k + P], WM["h"][:, s, P * k:P * k + P], ident)
                last.then_inc(G("m_htr"), 1)
                pe.wait_ge(G("m_hT"), i + 1)
                pe.wait_ge(G(f"ld_d{s}"), 16 * j + 16)
                if any_before:
                    pe.wait_ge(G("m_ya"), i)
                    pe.wait_ge(G("m_yd"), i)
                for h in range(2):
                    for k in range(KF):
                        last = mm(PS[:, 5 + h, :], WM["hT"][:, s, k, :], wd[s][:, k, 512 * h:512 * h + 512],
                                  start=(k == 0), stop=(k == KF - 1))
                last.then_inc(G("m_down"), 1)

            for s in range(2):
                item(0, s, True)
            with pe.Fori(1, pairs) as j:
                for s in range(2):
                    item(j, s, False)


_OUT = "out_dram"


def kernel(**inputs):
    import concourse.bacc as _bacc
    from concourse.bass_utils import run_bass_kernel_spmd as _run

    a = {k: np.asarray(v) for k, v in inputs.items()}

    def cols(v):
        return v.reshape(KD, P).T

    b = a["b_ada"][0].reshape(6, D)
    wr = np.concatenate([a["w_router_group"][0], a["w_router_expert"][0].transpose(1, 0, 2).reshape(D, NE)], 1)
    arrays = {
        "x": a["x"][0],
        "ccol": cols(a["c"][0]),
        "pos": a["positions"][0].reshape(T, P).T,
        "w_ada": a["w_ada"][0],
        "b_cols": np.stack([cols(b[1]), cols(b[0]), cols(b[4]), cols(b[3])], 1),
        "b_gt1": np.broadcast_to(b[2], (P, D)),
        "b_gt2": np.broadcast_to(b[5], (P, D)),
        "g_cols": np.stack([cols(a["g_norm_mix"][0]), cols(a["g_norm_ffn"][0])], 1),
        "g_final": np.broadcast_to(a["g_norm_final"], (P, D)),
        "w_in": a["w_in"][0],
        "w_o": a["w_o"][0],
        "w_router": wr.reshape(KD, P, 36).transpose(1, 0, 2).reshape(P, KD * 36),
        "w_up": a["w_up"][0],
        "w_gate": a["w_gate"][0],
        "w_down": a["w_down"][0],
        "const": CONST,
    }
    nc = _bacc.Bacc("TRN2", target_bir_lowering=False, num_devices=1)
    given, args = {}, {}
    for name, v in arrays.items():
        v = np.ascontiguousarray(v)
        given[f"in_{name}"] = v
        args[name] = nc.dram_tensor(f"in_{name}", v.shape, mybir.dt.from_np(v.dtype), kind="ExternalInput").ap()
    args["out"] = nc.dram_tensor(_OUT, (S, D), F32, kind="ExternalOutput").ap()
    block_kernel(nc, **args)
    r = _run(nc, [given], core_ids=[0])
    return r.results[0][_OUT].reshape(1, S, D)
```

```python
from contextlib import ExitStack

import numpy as np
import concourse.bass as bass
from concourse import mybir

F32 = mybir.dt.float32
F32R = mybir.dt.float32r
I32 = mybir.dt.int32
ALU = mybir.AluOpType
ACT = mybir.ActivationFunctionType
X_AXIS = mybir.AxisListType.X

P = 128
D = 1024
S = 1024
T = S // P
KD = D // P
HD = 64
HA, HB = 8, 8
NIH = 16
TOPK = 256
DMIX = 512
NG, EPG = 4, 8
NE = NG * EPG
FE = 512
KF = FE // P
EPS = 1e-6
D_IN = 4688
MAX_ITEMS = 2 * S // P + NE
HALF = KD * FE // 2
TBL = MAX_ITEMS + 2
NEG_SCORE = -3.0e38
A_SPEND = 4.0
V_SPEND = 7.0
B_SPEND = (6.0, 5.0, 6.0)
MIX_SPEND = 5.0
HEADS_SPEND = (2.4, 3.2, 0, 0, 0, 0, 0, 0)
TAKEN = -3.4e38
NEG_LOGIT = -1.0e30
ROUND = 12582912.0
TWO_PI = 2.0 * np.pi
PI_HI = 6.28125
PI_MID = float(np.float32(np.round((TWO_PI - PI_HI) * 2**20) / 2**20))
PI_LO = float(np.float32(TWO_PI - PI_HI - PI_MID))
PI_IN = 3.1415925

CHUNKS_A = (("qi0", 1536, 512), ("qi1", 2048, 512), ("kiwi", 2560, 80), ("qa", 0, 512),
            ("ka", 512, 512), ("va", 1024, 512))
NA1 = 3
CHUNKS_B = (("qb", 2640), ("kb", 3152), ("vb", 3664), ("gb", 4176))
FIRST_SCORED = TOPK // P
SCORED = range(FIRST_SCORED, T)
ACC_OFF = {i: sum(P * (j + 1) for j in SCORED if j < i) for i in SCORED}
ACC_ALL = sum(P * (j + 1) for j in SCORED)


def constant_table():
    p = np.arange(P)
    parts = {}
    parts["ident"] = np.eye(P)
    parts["before"] = (p[:, None] < p[None, :])
    parts["causal"] = (p[None, :] >= p[:, None])
    inv_a = np.float32(500000.0) ** (-np.arange(8, dtype=np.float32) / np.float32(8))
    inv_b = np.float32(10000.0) ** (-np.arange(32, dtype=np.float32) / np.float32(32))
    parts["invf"] = np.tile(np.concatenate([inv_a, inv_b])[None], (P, 1))
    lg = np.log1p(-np.exp2(-5.0 - np.arange(HB)))
    parts["kfac"] = np.exp(-(p[:, None] + 1.0) * lg[None]) * HD ** -0.5
    parts["xi"] = np.exp((p[:, None] + 1.0) * lg[None])
    parts["carry"] = np.tile(np.repeat(np.exp(P * lg), HD)[None], (P, 1))
    parts["unseen"] = np.tile(np.where(p < HD, 1.0, 0.0)[:, None], (1, HD))
    parts["desc"] = np.tile(np.arange(8, 0, -1)[None], (P, 1))
    parts["iota"] = np.tile(np.arange(P)[None], (P, 1))
    parts["even"] = np.tile(2 * np.arange(MAX_ITEMS // 2)[None], (P, 1))
    parts["token"] = p[:, None] + P * np.arange(T)[None]
    at, off = {}, 0
    for name, a in parts.items():
        at[name] = (off, off + a.shape[1])
        off += a.shape[1]
    return np.ascontiguousarray(np.concatenate([np.asarray(a, np.float32) for a in parts.values()], 1)), at


CONST, CONST_AT = constant_table()


class Own:

    def __init__(self, engine, step):
        self.engine, self.step, self.count = engine, step, {}
        self.last = None

    def go(self, instruction, sem=None):
        sem = sem or self.step
        instruction.then_inc(sem, 1)
        self.count[sem.name] = self.count.get(sem.name, 0) + 1
        self.last = (sem, self.count[sem.name])

    def wait(self):
        self.engine.wait_ge(*self.last)

    def __call__(self, instruction, sem=None):
        self.go(instruction, sem)
        self.wait()


def block_kernel(nc, x, ccol, pos, w_ada, b_cols, b_gt1, b_gt2, g_cols, g_final, w_in, w_o, w_router,
                 w_up, w_gate, w_down, const, out):
    ctx = ExitStack()
    with ctx:
        def sb(name, shape, dt=F32):
            return ctx.enter_context(nc.sbuf_tensor(name, shape, dt))

        def sem(name):
            return ctx.enter_context(nc.semaphore(name))

        def sems(name, n):
            return [sem(f"{name}{i}") for i in range(n)]

        q_dram = nc.dram_tensor("q_dram", (P, 4, S), F32).ap()
        yb_dram = nc.dram_tensor("yb_dram", (S, DMIX), F32).ap()
        x1_dram = nc.dram_tensor("x1_dram", (S, D), F32).ap()
        xn_dram = nc.dram_tensor("xn_dram", (S, D), F32).ap()
        y_dram = nc.dram_tensor("y_dram", (MAX_ITEMS * P, D), F32).ap()

        before = ExitStack()

        def sb_before(name, shape):
            return before.enter_context(nc.sbuf_tensor(name, shape, F32))

        BIG = sb_before("BIG", [P, 24576])
        hT = BIG[:, 0:8192].rearrange("p (k s) -> p k s", k=KD)
        ring = [BIG[:, 8192 + 4096 * i:8192 + 4096 * (i + 1)].rearrange("p (k c) -> p k c", k=KD) for i in range(2)]
        qiT = BIG[:, 16384:24576].rearrange("p (j s) -> p j s", j=8)
        ada_slot = [BIG[:, 8192:16384].rearrange("p (k c) -> p k c", k=KD),
                    BIG[:, 16384:24576].rearrange("p (k c) -> p k c", k=KD)]
        ada_late = [BIG[:, a:a + 4096].rearrange("p (k c) -> p k c", k=KD) for a in (0, 4096, 20480)]
        wb = [ring[0], ring[1],
              BIG[:, 16384:20480].rearrange("p (k c) -> p k c", k=KD),
              BIG[:, 20480:24576].rearrange("p (k c) -> p k c", k=KD)]
        wo = BIG[:, 8192:16384].rearrange("p (k c) -> p k c", k=KD)

        KV = sb_before("KV", [P, 8192 + 2048])
        kaT = KV[:, 0:4096].rearrange("p (j s) -> p j s", j=4)
        va = KV[:, 4096:8192].rearrange("p (t c) -> p t c", t=T)
        kiBD = KV[:, 8192:10240].rearrange("p (h s) -> p h s", h=2)
        xall = KV[:, 0:8192].rearrange("p (t d) -> p t d", t=T)
        ACC = sb_before("ACC", [P, ACC_ALL])
        before.close()
        raw = sb("raw", [P, 6, HALF])
        whi = sb("whi", [P, 4, HALF], F32R)
        wlo = sb("wlo", [P, 4, HALF], F32R)
        gt2 = sb("gt2", [P, D])[:, :]
        hhi = sb("hhi", [P, KF, P], F32R)
        hlo = sb("hlo", [P, KF, P], F32R)
        sb("spare", [P, 4096])
        xhi = sb("xhi", [P, 2, KD, P], F32R)
        xlo = sb("xlo", [P, 2, KD, P], F32R)
        sb("spare2", [P, ACC_ALL - 4096])

        cst = sb("cst", [P, CONST.shape[1]])
        ones = sb("ones", [P, P])
        WK = sb("WK", [P, 10000])
        late_sum = [BIG[:, a:a + 512] for a in (17408, 17920)] + [WK[:, 512 * m:512 * m + 512] for m in range(4)]

        def c(name):
            a, b = CONST_AT[name]
            return cst[:, a:b]

        ident = c("ident")
        cc = sb("cc", [P, KD])
        bc = sb("bc", [P, 4, KD])
        gc = sb("gc", [P, 2, KD])
        mod = sb("mod", [P, 4, KD])
        posi = sb("posi", [P, T], I32)
        posf = sb("posf", [P, T])
        tab = sb("tab", [P, 3, T, 40])
        wsc = sb("wsc", [P, T, NIH])
        zero = sb("zero", [P, 512])
        small = sb("small", [P, 64])
        expo = sb("expo", [P, 8])
        L = sb("L", [P, T, 36])

        cosT, sinT, nsinT = tab[:, 0], tab[:, 1], tab[:, 2]

        def work(spec):
            out_, off = {}, 0
            for name, shape in spec:
                n = int(np.prod(shape))
                v = WK[:, off:off + n]
                if len(shape) == 2:
                    v = v.rearrange("p (a b) -> p a b", a=shape[0])
                elif len(shape) == 3:
                    v = v.rearrange("p (a b c) -> p a b c", a=shape[0], b=shape[1])
                out_[name] = v
                off += n
            assert off <= 10000, off
            return out_

        W0 = work([("sq", (D,)), ("mac", (2, D)), ("dg", (512,)), ("ang", (T, 40)), ("k", (T, 40)), ("r", (T, 40)), ("c", (T, 40))])
        WA = work([("tmp", (3, 512)), ("s1", (128,)), ("s2", (128,)), ("trq", (2, 512)), ("R", (3, 1024))])
        WB = work([("qA", (2, 512)), ("kA", (2, 512)), ("qB", (512,)), ("kB", (512,)), ("v", (2, 512)),
                   ("g", (2, 512)), ("qBD", (4, 2, P)), ("kT", (4, P)), ("st", (4, P)),
                   ("y", (2, 512)), ("sq", (512,))])
        WB["S"] = KV[:, 8192:9216].rearrange("p (h n) -> p h n", h=HB)
        Wk = KV[:, 9216:10240]
        m8 = sb("m8", [P, 8])[:, :]
        WC = work([("sums", (4, 512)), ("S", (3, 1024)), ("PT", (2, 512)),
                   ("y", (512,)), ("yb", (512,)), ("yT", (8, P)), ("bias01", (256,)), ("wr", (8 * 36,)),
                   ("sq", (D,))])
        WC["q"] = BIG[:, 18432:20480].rearrange("p (s n) -> p s n", s=2)
        WC["gt1"] = KV[:, 8192:9216]
        WC["qBD"] = [WC["q"][:, s].rearrange("p (j h n) -> p j h n", j=4, h=2) for s in range(2)]
        WC["x"] = BIG[:, 16384:17408]
        WC["h2T"] = WC["yT"]
        WR = work([("e1", (T, NE)), ("e2", (T, NE)), ("A", (T, NE)), ("pre", (T, NE)), ("V", (T, NE)),
                   ("tmp", (T, NE)), ("f", (T, 8)), ("f2", (T, 8)), ("o1", (T, 8)), ("o2", (T, 8)),
                   ("ca", (T, 8)), ("G", (T, NG)), ("cg", (T, NG)), ("m", (T,)), ("gm", (T,)), ("t1", (T,)),
                   ("t2", (T,)), ("e2x", (T,)), ("cnt", (NE,)), ("nb", (NE,)), ("ends", (2, NE)), ("start", (NE,)),
                   ("row", (2, T)), ("q", (2, T)), ("r", (2, T)), ("h48", (48,)), ("it", (MAX_ITEMS * NE,)),
                   ("ohp", (2, P)), ("ohi", (2, 64)), ("ef", (64,)), ("h", (64,))])
        WM = work([("Xg", (2, D)), ("xT", (KD, P)), ("h", (FE,)), ("hs", (FE,)), ("Y", (2, D))])
        NF = 4
        raw_all = raw[:, :, :].rearrange("p q c -> p (q c)")
        WF = {name: [raw_all[:, D * (NF * n + s):D * (NF * n + s + 1)] for s in range(NF)]
              for n, name in enumerate(("y1", "y2"))}
        WF["sq"] = raw_all[:, 8 * D:9 * D]
        WF["x"] = [WK[:, 6144 + D * s:6144 + D * (s + 1)] for s in range(2)] + \
            [raw_all[:, D * s:D * (s + 1)] for s in (9, 10)]
        WF["gf"] = WK[:, 8192:8192 + D]
        sw = sb("sw", [P, 2, T])
        srow = sb("srow", [P, 2, T], I32)
        tbl = sb("tbl", [P, TBL], I32)
        gidx = sb("gidx", [P, 2 * NF], I32)
        ssum = sb("ssum", [P, 2, 8])
        nmax = sb("nmax", [P, 4])
        items = sb("items", [1, 64], I32)

        f_ms = [small[:, 55 + s:56 + s] for s in range(2)]
        f_rs = [small[:, 57 + s:58 + s] for s in range(2)]

        PS = ctx.enter_context(nc.psum_tensor("PS", [P, 8, 512], F32))

        class Signals:

            def __init__(self):
                self.made = {}

            def __call__(self, name):
                if name not in self.made:
                    self.made[name] = sem(name)
                return self.made[name]

        G = Signals()
        wada_v = w_ada.rearrange("(k p) (a c) -> p a k c", p=P, a=6)
        win_v = w_in.rearrange("(k p) c -> p k c", p=P)
        wo_v = w_o.rearrange("(k p) c -> p k c", p=P)
        x_v = x.rearrange("(t p) d -> t p d", p=P)
        wg_v = w_gate.rearrange("e (k p) f -> e p k f", p=P)
        wu_v = w_up.rearrange("e (k p) f -> e p k f", p=P)
        wd_v = w_down.rearrange("e (k p) f -> e p k f", p=P)
        NA = len(CHUNKS_A)
        UA = NA * T
        turned = [u for u in range(UA) if CHUNKS_A[u // T][0] != "va"]
        NTURN = len(turned)
        TURN1 = NA1 * T
        LATE = (("row", 2, 0), ("col", 4, 2), ("col", 3, 3), ("row", 5, 1))
        NU = len(SCORED) * NIH

        def cols_of(i):
            return P * (i + 1)

        def tile(t):
            return slice(P * t, P * (t + 1))

        order = []
        between = {i: [[("mix", i - 1)], [("norm", i - 1)], [("route", i - 1)], []] for i in range(1, T + 1)}
        between[0] = [[], [], [], []]
        between[1] = [[], [], [], [("mix", 0), ("norm", 0)]]
        between[2] = [[], [("late", 1), ("late", 2), ("route", 0), ("mix", 1)], [("norm", 1)], [("route", 1)]]
        for i in range(T + 1):
            for k in range(4):
                if i < T:
                    order.append(("heads", (i, 2 * k, 2 * k + 2)))
                order += between[i][k]
            if i < T:
                order.append(("rows", i))
            if i == 0:
                order.append(("late", 0))
            if i == T - 1:
                order.append(("late", 3))
        uses7 = []
        for kind, n in order:
            if kind == "late":
                uses7 += [("late", n, h) for h in range(2)]
            if kind == "mix":
                uses7 += [("mix", n, 0), ("mix", n, 1)]
            if kind == "route":
                uses7.append(("route", n, 0))
        at7 = {use: n for n, use in enumerate(uses7)}

        def groups(i):
            return (i + 4) // 4

        def pt_index(i, h, g):
            return HA * sum(groups(k) for k in range(i)) + h * groups(i) + g

        TAIL = 2
        GATE, DOWN, UP = (0, 1), (2, 3), (4, 5)

        def place(i, s, q):
            if s == TAIL:
                return 6 * i + (q - 4), q
            if isinstance(i, int) and i == 0:
                return (q, q) if q in GATE else (q - 2, q - 2)
            return 6 * i + (q - 2), (2 + 6 * s + q) % 4

        def known(i, below):
            return isinstance(i, int) and i < below

        PEELED = 3
        MOST_ROUNDS = (MAX_ITEMS - PEELED - 1) // 2

        def steps(engine, rounds, step):
            for i in range(PEELED):
                step(i, i % 2, False)
            with engine.Fori(0, rounds) as j:
                step(2 * j + PEELED, 1, False)
                step(2 * j + PEELED + 1, 0, False)
            step(2 * rounds + PEELED, 1, True)

        def count(rounds):
            return 2 * rounds + PEELED + 1

        block = ctx.enter_context(nc.Block())

        @block.sync
        def _(sp):
            for dst, src in ((cst[:, :], const), (cc[:, :], ccol), (bc[:, :, :], b_cols), (gc[:, :, :], g_cols),
                             (posi[:, :], pos)):
                sp.dma_start(dst, src).then_inc(G("ld_const"), 16)
            for t in range(T):
                sp.dma_start(xall[:, t, :], x_v[t]).then_inc(G(f"ld_x{t}"), 16)
            for s, part in enumerate((1, 0)):
                for h in range(2):
                    sp.dma_start(ada_slot[s][:, 4 * h:4 * h + 4], wada_v[:, part, 4 * h:4 * h + 4])\
                        .then_inc(G(f"slot{2 * s + h}"), 16)
            for n, (_, c0, w) in enumerate(CHUNKS_A):
                if n == 0:
                    sp.wait_ge(G("mac_done"), 1)
                if n >= 2:
                    sp.wait_ge(G("a_proj"), T * (n - 1))
                sp.dma_start(ring[n % 2][:, :, 0:w], win_v[:, :, c0:c0 + w]).then_inc(G(f"ld_w{n % 2}"), 16)
                if n == NA1 + 1:
                    sp.wait_ge(G("sc_ready"), NU)
                    for k in (2, 3):
                        sp.dma_start(wb[k], win_v[:, :, CHUNKS_B[k][1]:CHUNKS_B[k][1] + 512])\
                            .then_inc(G(f"ld_wb{k}"), 16)
            for k in (0, 1):
                sp.wait_ge(G("a_proj"), UA - T * (1 - k))
                sp.dma_start(wb[k], win_v[:, :, CHUNKS_B[k][1]:CHUNKS_B[k][1] + 512]).then_inc(G(f"ld_wb{k}"), 16)

            def load_queries(n):
                for h in range(2):
                    sp.dma_start(WC["qBD"][n % 2][64 * h:64 * h + 64, :, h, :],
                                 q_dram[64 * h:64 * h + 64, :, tile(n)]).then_inc(G(f"ld_q{n % 2}"), 16)

            for t in range(T):
                if t == T - 1:
                    sp.wait_ge(G("b_proj"), 4 * T)
                    sp.wait_ge(G("q_clear"), 1)
                    for q in range(2):
                        sp.wait_ge(G(f"st_q{q}"), 16 * (T // 2))
                    for n in range(2):
                        load_queries(n)
                    sp.dma_start(wo, wo_v).then_inc(G("ld_wo"), 16)
                sp.wait_ge(G("b_out"), t + 1)
                sp.dma_start(yb_dram[tile(t), :], WB["y"][:, t % 2]).then_inc(G(f"st_yb{t % 2}"), 16)
            sp.wait_ge(G("b_qr"), T)
            sp.wait_ge(G("b_kr"), T)
            sp.dma_start(WC["gt1"], b_gt1).then_inc(G("ld_c"), 16)
            sp.dma_start(WC["wr"], w_router).then_inc(G("ld_c"), 16)
            sp.wait_ge(G("st_yb0"), 16 * (T // 2))
            sp.wait_ge(G("st_yb1"), 16 * (T // 2))
            for i in range(T):
                if 1 <= i < T - 1:
                    sp.wait_ge(G("c_qk"), HA * i)
                    load_queries(i + 1)
                if i >= 1:
                    sp.wait_ge(G("c_ytr"), i)
                sp.dma_start(WC["yb"], yb_dram[tile(i), :]).then_inc(G("ld_yb"), 16)
                if i >= 1:
                    sp.wait_ge(G("c_x1"), i)
                    sp.dma_start(x1_dram[tile(i - 1), :], WC["x"]).then_inc(G("st_x1"), 16)
                    sp.wait_ge(G("c_xn"), i)
                    sp.dma_start(xn_dram[tile(i - 1), :], WC["sq"]).then_inc(G("st_xn"), 16)
                    sp.wait_ge(G("st_x1"), 16 * i)
                sp.dma_start(WC["x"], x_v[i]).then_inc(G("ld_xr"), 16)
            sp.wait_ge(G("c_pv"), pt_index(T - 1, HA - 1, groups(T - 1) - 1) + 1)
            sp.dma_start(gt2, b_gt2).then_inc(G("ld_gt2"), 16)
            sp.wait_ge(G("c_x1"), T)
            sp.dma_start(x1_dram[tile(T - 1), :], WC["x"]).then_inc(G("st_x1"), 16)
            sp.wait_ge(G("c_xn"), T)
            sp.dma_start(xn_dram[tile(T - 1), :], WC["sq"]).then_inc(G("st_xn"), 16)
            sp.wait_ge(G("st_x1"), 16 * T)
            sp.wait_ge(G("r_items"), 1)
            sp.wait_ge(G("b7_ready"), len(uses7))
            rounds = nc.sync.value_load(items[0:1, 63:64], min_val=1, max_val=MOST_ROUNDS)

            def half(item, i, s, q):
                expert = nc.sync.value_load(items[0:1, item:item + 1] if isinstance(item, int) else
                                            items[0:1, bass.ds(item, 1)], min_val=0, max_val=NE - 1)
                src = (wg_v, wd_v, wu_v)[q // 2][bass.ds(expert, 1)].squeeze(0)
                h = q % 2
                if q in DOWN:
                    src, dst = src[:, 2 * h:2 * h + 2], raw[:, q].rearrange("p (k c) -> p k c", k=2)
                else:
                    src, dst = src[:, 4 * h:4 * h + 4], raw[:, q].rearrange("p (k c) -> p k c", k=4)
                if not known(i, 1) and not (known(i, 2) and q in DOWN):
                    sp.wait_ge(G("m_lo"), place(i - 1, 0, q)[0] + 1)
                sp.dma_start(dst, src).then_inc(G(f"ld_e{q}"), 16)

            def step(i, s, last):
                for q in GATE:
                    half(i, i, s, q)
                if not known(i, 1):
                    for q in DOWN:
                        half(i - 1, i, s, q)
                for q in UP:
                    half(i, i, s, q)
                if known(i, 1):
                    sp.wait_ge(G("r_done"), 1)
                    sp.dma_start(WF["gf"], g_final).then_inc(G("ld_gf"), 16)
                    for t in range(2):
                        sp.dma_start(WF["x"][t], x1_dram[tile(t), :]).then_inc(G(f"ld_x{t}"), 16)

            steps(sp, rounds, step)
            for q in DOWN:
                half(count(rounds) - 1, count(rounds), TAIL, q)
            sp.wait_ge(G("m_end"), 1)
            for t in range(2, NF):
                sp.dma_start(WF["x"][t], x1_dram[tile(t), :]).then_inc(G(f"ld_x{t}"), 16)
            for t in range(T):
                sp.wait_ge(G("f_out"), t + 1)
                sp.dma_start(out[tile(t), :], WF["x"][t % NF]).then_inc(G(f"slot{t % NF}"), 16)
                n = t - 1 + NF
                if NF <= n < T:
                    sp.wait_ge(G(f"slot{n % NF}"), 16 + 16 * (n // NF))
                    sp.dma_start(WF["x"][n % NF], x1_dram[tile(n), :]).then_inc(G(f"ld_x{n}"), 16)
            for s in range(NF):
                sp.wait_ge(G(f"slot{s}"), 16 + 16 * (T // NF))

        @block.gpsimd
        def _(pool):
            own = Own(pool, G("pool_step"))
            tt = nc.gpsimd.tensor_tensor
            own.go(nc.gpsimd.memset(expo[:, :], -0.5))
            own(nc.gpsimd.memset(zero[:, :], 0.0), G("pool_zeros"))
            own(nc.gpsimd.memset(ones[:, :], 1.0), G("pool_ones"))
            own(nc.gpsimd.memset(KV[:, 8192:10240], 0.0), G("pool_zero"))
            pool.wait_ge(G("dve_ms"), 1)
            own(tt(small[:, 8:16], small[:, 0:8], expo[:, :], ALU.pow), G("pool_rstd"))
            for t in range(T):
                pool.wait_ge(G("a_evac"), TURN1 + t + 1)
                pool.dma_start(q_dram[:, :, tile(t)], WA["trq"][:, t % 2].rearrange("p (j s) -> p j s", j=4))\
                    .then_inc(G(f"st_q{t % 2}"), 16)
            pool.wait_ge(G("sc_acc"), NU)
            for q in range(2):
                pool.wait_ge(G(f"st_q{q}"), 16 * (T // 2))
            own(nc.gpsimd.memset(WB["qBD"].rearrange("p j h n -> p (j h n)"), 0.0), G("b_clear"))

            def b_root(t):
                pool.wait_ge(G("b_ms"), t + 1)
                own(tt(small[:, 40:48], small[:, 32:40], expo[:, :], ALU.pow), G("b_rs"))

            for t in range(T):
                q_, k_ = WB["qA"][:, t % 2], WB["kA"][:, t % 2]
                k3 = k_.rearrange("p (h d) -> p h d", h=HB)
                pool.wait_ge(G("b_qsplit"), t + 1)
                own(tt(q_, q_, WB["qB"], ALU.add), G("b_qr"))
                pool.wait_ge(G("b_ksplit"), t + 1)
                own(tt(k_, k_, WB["kB"], ALU.add))
                own(tt(k3, k3, c("kfac").unsqueeze(2).to_broadcast([P, HB, HD]), ALU.mult), G("b_kr"))
                if t >= 1:
                    b_root(t - 1)

            def load_late(m):
                n, h = divmod(m, 2)
                if m >= 3:
                    pool.wait_ge(G("late_sum"), m - 2)
                pool.dma_start(ada_late[m % 3], wada_v[:, LATE[n][1], :, 512 * h:512 * h + 512])\
                    .then_inc(G(f"ld_late{m % 3}"), 16)

            pool.wait_ge(G("b_proj"), 4 * T)
            own(nc.gpsimd.memset(WC["q"], 0.0), G("q_clear"))
            for m in range(3):
                load_late(m)
            b_root(T - 1)
            pool.wait_ge(G("b_out"), T)
            pool.wait_ge(G("b_y"), T)
            own(nc.gpsimd.memset(WC["bias01"], 0.0), G("c_clear"))
            for kind, n in order:
                for m in {("late", 0): (3, 4), ("mix", 0): (5,), ("late", 1): (6,), ("late", 2): (7,)}.get((kind, n), ()):
                    load_late(m)
                if kind == "norm":
                    pool.wait_ge(G("c_ms"), n + 1)
                    own(tt(small[:, 49:50], small[:, 48:49], expo[:, 0:1], ALU.pow), G("c_rs"))
            pool.wait_ge(G("r_done"), 1)
            pool.wait_ge(G("st_xn"), 16 * T)
            rounds = nc.gpsimd.value_load(items[0:1, 63:64], min_val=1, max_val=MOST_ROUNDS)

            def take_index(column, s):
                nc.gpsimd.tensor_copy(gidx[:, s:s + 1], column).then_inc(G("m_idx"), 1)

            def gather(s):
                nc.gpsimd.indirect_dma_start(
                    out=WM["Xg"][:, s], out_offset=None, in_=xn_dram,
                    in_offset=bass.IndirectOffsetOnAxis(ap=gidx[:, s:s + 1], axis=0)).then_inc(G(f"ld_rows{s}"), 16)

            for i in range(2):
                take_index(tbl[:, i:i + 1], i)
            pool.wait_ge(G("m_idx"), 2)
            gather(0)

            def step(i, s, last):
                if not last:
                    pool.wait_ge(G("m_idx"), i + 2)
                    if not known(i, 1):
                        pool.wait_ge(G("m_xtr"), i)
                    pool.wait_ge(G(f"ld_rows{s}"), 8 * (i - s) + 16)
                    take_index(tbl[:, i + 2:i + 3] if known(i, PEELED) else tbl[:, bass.ds(i + 2, 1)], s)
                    gather(1 - s)
                pool.wait_ge(G("m_xhi"), i + 1)
                nc.gpsimd.tensor_tensor(xlo[:, s], WM["xT"], xhi[:, s].bitcast(F32), ALU.subtract)\
                    .then_inc(G("m_xlo"), 1)

            steps(pool, rounds, step)
            pool.wait_ge(G("m_end"), 1)

            def f_root(t):
                pool.wait_ge(G("f_ms"), t + 1)
                own(tt(f_rs[t % 2], f_ms[t % 2], expo[:, 0:1], ALU.pow), G("f_rs"))

            def gather_pair(t):
                s = t % NF
                if t >= NF:
                    pool.wait_ge(G("f_sum"), t - NF + 1)
                for e, name in enumerate(("y1", "y2")):
                    column = gidx[:, 2 * s + e:2 * s + e + 1]
                    own(nc.gpsimd.tensor_copy(column, srow[:, e, t:t + 1]))
                    nc.gpsimd.indirect_dma_start(
                        out=WF[name][s], out_offset=None, in_=y_dram,
                        in_offset=bass.IndirectOffsetOnAxis(ap=column, axis=0)).then_inc(G(f"f_y{s}"), 16)

            for t in range(NF - 1):
                gather_pair(t)
            for t in range(T):
                if t + NF - 1 < T:
                    gather_pair(t + NF - 1)
                f_root(t)

        @block.scalar
        def _(act):
            own = Own(act, G("act_step"))
            A = nc.scalar.activation
            for t in range(T):
                act.wait_ge(G(f"ld_x{t}"), 16)
                own(A(W0["sq"], xall[:, t, :], ACT.Square, accum_out=small[:, 16 + t:17 + t]), G("act_sq"))
            act.wait_ge(G("rope_arg"), 1)

            def flat(a):
                return a.rearrange("p t f -> p (t f)")

            own.go(A(flat(sinT), flat(W0["r"]), ACT.Sin))
            own.go(A(flat(nsinT), flat(W0["r"]), ACT.Sin, scale=-1.0))
            own(A(flat(cosT), flat(W0["c"]), ACT.Sin), G("rope_tab"))
            for t in range(T):
                act.wait_ge(G("xt_ready"), t + 1)
                b = 4 + 2 * (t % 2)
                own.go(A(hT[:, :, tile(t)], PS[:, b:b + 2, :].rearrange("p b (k n) -> p (b k) n", k=4), ACT.Copy),
                       G("hT_raw"))
            act.wait_ge(G("pool_zeros"), 1)

            def zero_rows(n):
                n, h = divmod(n, 2)
                rows = slice(n * MAX_ITEMS // 4 * P, (n + 1) * MAX_ITEMS // 4 * P)
                act.dma_start(y_dram[rows, 512 * h:512 * h + 512].rearrange("(i p) c -> p i c", p=P),
                              zero[:, :].unsqueeze(1).to_broadcast([P, MAX_ITEMS // 4, 512]))\
                    .then_inc(G(f"st_y{h}"), 16)


            def a_copy(u):
                name, _, w = CHUNKS_A[u // T]
                t = u % T
                act.wait_ge(G("a_proj"), u + 1)
                if name == "va":
                    dst = va[:, t, :]
                    act.wait_ge(G("xt_ready"), T)
                else:
                    m = turned.index(u)
                    if m >= 3:
                        act.wait_ge(G("a_tr"), m - 2)
                    dst = WA["tmp"][:, m % 3, 0:w]
                own.go(A(dst, PS[:, u % 4, 0:w], ACT.Copy), G("a_copied"))

            for u in range(NA1 * T):
                a_copy(u)
                if T <= u < T + 8:
                    zero_rows(u - T)
            for u in range(NU):
                K = cols_of(FIRST_SCORED + u // NIH)
                b = 2 * (u % 3)
                act.wait_ge(G("sc_ready"), u + 1)
                if u >= 3:
                    act.wait_ge(G("sc_acc"), u - 2)
                own.go(A(WA["R"][:, u % 3, 0:K], PS[:, b:b + 2, :].rearrange("p b c -> p (b c)")[:, 0:K], ACT.Relu),
                       G("sc_relu"))
            for u in range(NA1 * T, UA):
                a_copy(u)

            def b_evacuate(t):
                act.wait_ge(G("b_trq"), t + 1)
                if t == 0:
                    act.wait_ge(G("b_clear"), 1)
                pq = PS[:, 4, :].rearrange("p (j n) -> p j n", j=4)
                own.go(A(WB["qBD"][0:64, :, 0, :], pq[0:64], ACT.Copy))
                own.go(A(WB["qBD"][64:128, :, 1, :], pq[64:128], ACT.Copy), G("b_qbd"))
                act.wait_ge(G("b_trk"), t + 1)
                own.go(A(WB["kT"], PS[:, 5, :].rearrange("p (j n) -> p j n", j=4), ACT.Copy), G("b_kT"))

            act.wait_ge(G("sc_acc"), NU)
            for t in range(T):
                act.wait_ge(G("b_proj"), 4 * t + 3)
                if t >= 2:
                    act.wait_ge(G("b_y"), t - 1)
                    act.wait_ge(G("b_out"), t - 1)
                own.go(A(WB["v"][:, t % 2], PS[:, 2, :], ACT.Copy), G("b_v"))
                act.wait_ge(G("b_proj"), 4 * t + 4)
                own.go(A(WB["g"][:, t % 2], PS[:, 3, :], ACT.Silu), G("b_g"))
                if t >= 1:
                    b_evacuate(t - 1)
            b_evacuate(T - 1)
            act.wait_ge(G("c_clear"), 1)
            for kind, i in order:
                if kind == "heads":
                    i, lo, hi = i
                    K = cols_of(i)
                    for h in range(lo, hi + 1):
                        u = HA * i + h
                        if h < hi:
                            act.wait_ge(G("c_soft"), u + 1)
                            S_ = WC["S"][:, u % 3, 0:K]
                            own.go(A(S_, S_, ACT.Exp, bias=nmax[:, u % 4:u % 4 + 1], scale=-1.0,
                                     accum_out=ssum[:, i % 2, h:h + 1]), G("c_exp"))
                        if h > lo:
                            for g in range(groups(i)):
                                n = pt_index(i, h - 1, g)
                                w = min(512, K - 512 * g)
                                act.wait_ge(G("c_tr"), n + 1)
                                if n >= 2:
                                    act.wait_ge(G("c_pv"), n - 1)
                                own.go(A(WC["PT"][:, n % 2, 0:w], PS[:, 4 + n % 2, 0:w], ACT.Copy), G("c_pt"))
                if kind == "mix":
                    act.wait_ge(G("c_ytr"), i + 1)
                    own.go(A(WC["yT"], PS[:, 4:6, :].rearrange("p b (k n) -> p (b k) n", k=4), ACT.Copy), G("c_yT"))
                if kind == "norm":
                    act.wait_ge(G("c_x1"), i + 1)
                    if i >= 1:
                        act.wait_ge(G("st_xn"), 16 * i)
                        act.wait_ge(G("c_htr"), i)
                    own.go(A(WC["sq"], WC["x"], ACT.Square, accum_out=small[:, 52:53]), G("c_sq"))
            act.wait_ge(G("r_arg"), 1)
            own.go(A(flat(WR["cg"]), flat(WR["cg"]), ACT.Exp))
            own(A(WR["e2x"], WR["e2x"], ACT.Exp), G("r_exp"))
            act.wait_ge(G("r_done"), 1)
            rounds = nc.scalar.value_load(items[0:1, 63:64], min_val=1, max_val=MOST_ROUNDS)

            def high(i, s, q):
                n, slot = place(i, s, q)
                act.wait_ge(G(f"ld_e{q}"), 16 * i + 16 if q not in DOWN else 16 * i)
                if not (isinstance(n, int) and n < 4):
                    act.wait_ge(G("m_used"), n - 3)
                nc.scalar.activation(whi[:, slot], raw[:, q], ACT.Copy).then_inc(G("m_hi"), 1)

            def high_rows(i, s):
                act.wait_ge(G("m_xm"), i + 1)
                nc.scalar.activation(xhi[:, s], WM["xT"], ACT.Copy).then_inc(G("m_xhi"), 1)

            def down_half(i, s, after):
                act.wait_ge(G("m_used"), after + 1)
                act.wait_ge(G(f"st_y{s}"), 8 * (i - s) + 64)
                nc.scalar.activation(WM["Y"][:, s, 0:512], PS[:, 5, :], ACT.Copy).then_inc(G("m_ya"), 1)

            def store(i, s):
                act.wait_ge(G("m_ya"), i + 1)
                act.wait_ge(G("m_yd"), i + 1)
                rows = slice(i * P, (i + 1) * P) if known(i, PEELED) else bass.ds(i * P, P)
                act.dma_start(y_dram[rows, :], WM["Y"][:, s]).then_inc(G(f"st_y{s}"), 16)

            def high_hidden(i):
                act.wait_ge(G("m_htr"), i + 1)
                nc.scalar.activation(hhi[:, :, :], PS[:, 4, :].rearrange("p (k n) -> p k n", k=KF), ACT.Copy)\
                    .then_inc(G("m_hhi"), 1)

            def step(i, s, last):
                if not known(i, 1):
                    high_hidden(i - 1)
                high(i, s, UP[0])
                act.wait_ge(G("m_used"), place(i, s, GATE[1])[0] + 1)
                if not known(i, 1):
                    act.wait_ge(G("m_h"), i)
                nc.scalar.activation(WM["hs"], PS[:, 2, :], ACT.Silu).then_inc(G("m_silu"), 1)
                high(i, s, UP[1])
                if not last:
                    high_rows(i + 1, 1 - s)
                    high(i + 1, 1 - s, GATE[0])
                if not known(i, 1):
                    down_half(i - 1, 1 - s, place(i, s, DOWN[1])[0])
                if not last:
                    high(i + 1, 1 - s, GATE[1])
                if not known(i, 1):
                    store(i - 1, 1 - s)
                for q in DOWN:
                    high(i + 1, TAIL if last else 1 - s, q)

            high_rows(0, 0)
            for q in GATE:
                high(0, 0, q)
            steps(act, rounds, step)
            high_hidden(count(rounds) - 1)
            down_half(count(rounds) - 1, 1, place(count(rounds), TAIL, DOWN[1])[0])
            store(count(rounds) - 1, 1)
            act.wait_ge(G("st_y0"), 8 * count(rounds) + 64)
            act.wait_ge(G("st_y1"), 8 * count(rounds) + 64)
            own(A(small[:, 62:63], expo[:, 0:1], ACT.Copy), G("m_end"))
            def f_scale(t):
                act.wait_ge(G(f"f_y{t % NF}"), 32 * (t // NF + 1))
                y1 = WF["y1"][t % NF]
                own(A(y1, y1, ACT.Copy, scale=sw[:, 0, t:t + 1]), G("f_scaled"))

            f_scale(0)
            for t in range(T):
                if t < T - 1:
                    f_scale(t + 1)
                act.wait_ge(G("f_sum"), t + 1)
                own(A(WF["sq"], WF["x"][t % NF], ACT.Square, accum_out=small[:, 53 + t % 2:54 + t % 2]), G("f_sq"))

        @block.vector
        def _(dve):
            own = Own(dve, G("dve_step"))
            V = nc.vector

            def modulate(dst, banks, which):
                for k in range(KD):
                    yield V.tensor_scalar(dst[:, k], PS[:, banks + k // 4, P * (k % 4):P * (k % 4) + P],
                                          mod[:, 2 * which, k:k + 1], mod[:, 2 * which + 1, k:k + 1], ALU.mult,
                                          ALU.add)

            def modulate_all(dst, banks, which, signal):
                for k, ins in enumerate(modulate(dst, banks, which)):
                    own.go(ins, signal if k == KD - 1 else None)

            def own_columns(bank, scratch, at, h, signal):
                s3 = scratch.rearrange("p (k n) -> p k n", k=4)
                own(V.tensor_tensor(s3, PS[:, bank, :].rearrange("p (k n) -> p k n", k=4),
                                    ident.unsqueeze(1).to_broadcast([P, 4, P]), ALU.mult), signal)
                part = mod[:, at, 4 * h:4 * h + 4]
                own(V.tensor_reduce(part, s3, X_AXIS, ALU.add))
                own(V.tensor_tensor(part, part, bc[:, at, 4 * h:4 * h + 4], ALU.add))

            dve.wait_ge(G("ld_const"), 16 * 5)
            own(V.tensor_copy(posf[:, :], posi[:, :]))
            own(V.tensor_tensor(W0["ang"], posf[:, :].unsqueeze(2).to_broadcast([P, T, 40]),
                                c("invf").unsqueeze(1).to_broadcast([P, T, 40]), ALU.mult))
            own(V.tensor_scalar(W0["k"], W0["ang"], 1.0 / TWO_PI, ROUND, ALU.mult, ALU.add))
            own(V.tensor_scalar(W0["k"], W0["k"], ROUND, None, ALU.subtract))
            for part in (PI_HI, PI_MID, PI_LO):
                own(V.scalar_tensor_tensor(W0["ang"], W0["k"], -part, W0["ang"], ALU.mult, ALU.add))
            own(V.tensor_scalar(W0["r"], W0["ang"], PI_IN, -PI_IN, ALU.min, ALU.max))
            own(V.tensor_scalar(W0["c"], W0["ang"], TWO_PI / 4, None, ALU.add))
            own(V.tensor_scalar(W0["k"], W0["c"], TWO_PI / 2, -TWO_PI, ALU.is_gt, ALU.mult))
            own(V.tensor_tensor(W0["c"], W0["c"], W0["k"], ALU.add))
            own(V.tensor_scalar(W0["c"], W0["c"], PI_IN, -PI_IN, ALU.min, ALU.max), G("rope_arg"))
            dve.wait_ge(G("act_sq"), T)
            own(V.tensor_scalar(small[:, 0:8], small[:, 16:24], 1.0 / D, EPS, ALU.mult, ALU.add), G("dve_ms"))
            dve.wait_ge(G("pool_rstd"), 1)
            for t in range(T):
                own.go(V.tensor_scalar(xall[:, t, :], xall[:, t, :], small[:, 8 + t:9 + t], None, ALU.mult),
                       G("xn_ready"))
            for n in range(2 * KD):
                s, k = divmod(n, KD)
                mac = W0["mac"][:, s]
                if n % 4 == 0:
                    dve.wait_ge(G(f"slot{n // 4}"), 16)
                if k == 0:
                    own(V.tensor_scalar(mac, ada_slot[s][:, k], cc[:, k:k + 1], None, ALU.mult), G("mac_part"))
                else:
                    own(V.scalar_tensor_tensor(mac, ada_slot[s][:, k], cc[:, k:k + 1], mac, ALU.mult, ALU.add),
                        G("mac_done") if k == KD - 1 else None)
                if n == KD + 3:
                    dve.wait_ge(G("pe_cols"), 1)
                    for h in range(2):
                        own_columns(h, W0["dg"], 0, h, None)
            dve.wait_ge(G("pe_cols"), 2)
            for h in range(2):
                own_columns(2 + h, W0["dg"], 1, h, None)
            own(V.scalar_tensor_tensor(mod[:, 0, :], mod[:, 0, :], 1.0, gc[:, 0, :], ALU.add, ALU.mult))
            dve.wait_ge(G("hT_raw"), T)
            for half in range(2):
                for k in range(KD):
                    part = hT[:, k, 512 * half:512 * half + 512]
                    own.go(V.tensor_scalar(part, part, mod[:, 0, k:k + 1], mod[:, 1, k:k + 1], ALU.mult, ALU.add),
                           G("hT_ready") if k == KD - 1 else None)

            def rotate_part(v, t, heads):
                n = 16 * heads
                s1 = WA["s1"][:, 0:n].rearrange("p (h a d) -> p h a d", h=heads, a=2)
                s2 = WA["s2"][:, 0:n].rearrange("p (h a d) -> p h a d", h=heads, a=2)
                wide = [P, heads, 2, 8]
                half = [P, heads, 8]
                own.go(V.tensor_tensor(s1, v, cosT[:, t, 0:8].unsqueeze(1).unsqueeze(1).to_broadcast(wide),
                                       ALU.mult))
                own.go(V.tensor_tensor(s2[:, :, 0], v[:, :, 1], nsinT[:, t, 0:8].unsqueeze(1).to_broadcast(half),
                                       ALU.mult))
                own(V.tensor_tensor(s2[:, :, 1], v[:, :, 0], sinT[:, t, 0:8].unsqueeze(1).to_broadcast(half),
                                    ALU.mult))
                return V.tensor_tensor(v, s1, s2, ALU.add)

            def a_evacuate(m):
                u = turned[m]
                name, t = CHUNKS_A[u // T][0], u % T
                dve.wait_ge(G("a_tr"), m + 1)
                bank = PS[:, 4 + m % 2, :].rearrange("p (j n) -> p j n", j=4)
                if name == "qa":
                    if t >= 2:
                        dve.wait_ge(G(f"st_q{t % 2}"), 16 * (t // 2))
                    ins = V.tensor_copy(WA["trq"][:, t % 2].rearrange("p (j n) -> p j n", j=4), bank)
                elif name == "ka":
                    ins = V.tensor_copy(kaT[:, :, tile(t)], bank)
                elif name in ("qi0", "qi1"):
                    j = 4 * int(name[2])
                    ins = V.tensor_copy(qiT[:, j:j + 4, tile(t)], bank)
                else:
                    own.go(V.tensor_copy(kiBD[0:64, 0, tile(t)], bank[0:64, 0]))
                    ins = V.tensor_copy(kiBD[64:128, 1, tile(t)], bank[64:128, 0])
                own.go(ins, G("a_evac"))

            dve.wait_ge(G("rope_tab"), 1)
            dve.wait_ge(G("pool_zero"), 1)

            def a_rotate(m):
                u = turned[m]
                name, t = CHUNKS_A[u // T][0], u % T
                tmp = WA["tmp"][:, m % 3]
                dve.wait_ge(G("a_copied"), u + 1)
                if name == "kiwi":
                    own.go(V.tensor_scalar(wsc[:, t, :], tmp[:, 64:80], NIH ** -0.5 * HD ** -0.5, None, ALU.mult))
                    own(rotate_part(tmp[:, 0:16].rearrange("p (h a d) -> p h a d", h=1, a=2), t, 1))
                    own(V.tensor_copy(tmp[:, 64:128], tmp[:, 0:64]), G("a_rot"))
                else:
                    v = tmp.rearrange("p (h c) -> p h c", h=8)[:, :, 0:16].rearrange("p h (a d) -> p h a d", a=2)
                    own(rotate_part(v, t, 8), G("a_rot"))

            for m in range(TURN1):
                a_rotate(m)
                if m >= 1:
                    a_evacuate(m - 1)
            a_evacuate(TURN1 - 1)
            own.wait()
            for u in range(NU):
                i, h = FIRST_SCORED + u // NIH, u % NIH
                K = cols_of(i)
                acc = ACC[:, ACC_OFF[i]:ACC_OFF[i] + K]
                R = WA["R"][:, u % 3, 0:K]
                dve.wait_ge(G("sc_relu"), u + 1)
                if h == 0:
                    own(V.tensor_scalar(acc, R, wsc[:, i, h:h + 1], None, ALU.mult), G("sc_acc"))
                else:
                    own(V.scalar_tensor_tensor(acc, R, wsc[:, i, h:h + 1], acc, ALU.mult, ALU.add), G("sc_acc"))
                if h == NIH - 1:
                    own(V.scalar_tensor_tensor(acc[:, K - 64:K], c("unseen"), NEG_SCORE, acc[:, K - 64:K], ALU.mult,
                                               ALU.add))

            def top_k():
                for i in SCORED:
                    K = cols_of(i)
                    acc = ACC[:, ACC_OFF[i]:ACC_OFF[i] + K]
                    own(V.tensor_copy(Wk[:, 0:K], acc))
                    for _ in range(TOPK // 8):
                        own(V.max(m8, Wk[:, 0:K]))
                        own(V.match_replace(Wk[:, 0:K], m8, Wk[:, 0:K], TAKEN))
                        yield 2 * K / 960 + 0.2
                    own(V.tensor_tensor(acc, acc, Wk[:, 0:K], ALU.is_equal))
                    own(V.tensor_scalar(acc, acc, NEG_LOGIT, None, ALU.mult), G("topk_done"))
                    yield K / 640 + 0.2

            summed = []

            def late_sums(parts):
                for m in parts:
                    w_, total = ada_late[m % 3], late_sum[m % 6]
                    dve.wait_ge(G(f"ld_late{m % 3}"), 16 * (m // 3 + 1))
                    if m >= 6:
                        dve.wait_ge(G("b7_ready"), at7[("late", 0, m % 2)] + 1)
                    for k in range(KD):
                        if k == 0:
                            own(V.tensor_scalar(total, w_[:, 0], cc[:, 0:1], None, ALU.mult))
                        else:
                            own(V.scalar_tensor_tensor(total, w_[:, k], cc[:, k:k + 1], total, ALU.mult, ALU.add),
                                G("late_sum") if k == KD - 1 else None)
                        if k == KD - 1:
                            summed.append(m)
                        yield 0.8

            def late_work():
                yield from late_sums(range(6))
                yield from pieces
                yield from late_sums(range(6, 8))

            def sum_up(n):
                while len(summed) < n:
                    next(last_pieces)

            pieces = top_k()
            last_pieces = late_work()

            def spend(cost, work_left=pieces):
                while cost > 0:
                    took = next(work_left, None)
                    if took is None:
                        return
                    cost -= took

            for m in range(TURN1, NTURN):
                a_rotate(m)
                spend(A_SPEND)
                if m > TURN1:
                    a_evacuate(m - 1)
            a_evacuate(NTURN - 1)
            own.wait()
            spend(V_SPEND * T)

            def b_rotate(t):
                for bank, a, b, signal in ((0, WB["qA"][:, t % 2], WB["qB"], "b_qsplit"),
                                           (1, WB["kA"][:, t % 2], WB["kB"], "b_ksplit")):
                    dve.wait_ge(G("b_proj"), 4 * t + bank + 1)
                    if t >= 1:
                        dve.wait_ge(G("b_qr" if bank == 0 else "b_kr"), t)
                    if t >= 2:
                        dve.wait_ge(G("b_y"), t - 1)
                    src = PS[:, bank, :].rearrange("p (h a d) -> p h a d", h=HB, a=2)
                    a4 = a.rearrange("p (h a d) -> p h a d", h=HB, a=2)
                    b4 = b.rearrange("p (h a d) -> p h a d", h=HB, a=2)
                    half = [P, HB, 32]
                    own.go(V.tensor_tensor(a4, src, cosT[:, t, 8:40].unsqueeze(1).unsqueeze(1)
                                           .to_broadcast([P, HB, 2, 32]), ALU.mult))
                    own.go(V.tensor_tensor(b4[:, :, 0], src[:, :, 1],
                                           nsinT[:, t, 8:40].unsqueeze(1).to_broadcast(half), ALU.mult))
                    own.go(V.tensor_tensor(b4[:, :, 1], src[:, :, 0],
                                           sinT[:, t, 8:40].unsqueeze(1).to_broadcast(half), ALU.mult), G(signal))

            def b_retain(t):
                dve.wait_ge(G("b_s"), t + 1)
                if t >= 1:
                    dve.wait_ge(G("b_y"), t)
                for half in range(2):
                    own.go(V.tensor_tensor(WB["S"][:, 4 * half:4 * half + 4],
                                           PS[:, 6 + half, :].rearrange("p (h n) -> p h n", h=4),
                                           c("causal").unsqueeze(1).to_broadcast([P, 4, P]), ALU.mult),
                           G("b_sm") if half else None)
                spend(B_SPEND[1])
                dve.wait_ge(G("b_y"), t + 1)
                if t >= 2:
                    dve.wait_ge(G(f"st_yb{t % 2}"), 16 * (t // 2))
                y = WB["y"][:, t % 2]
                y3 = y.rearrange("p (h d) -> p h d", h=HB)
                sq3 = WB["sq"].rearrange("p (h d) -> p h d", h=HB)
                per = [P, HB, HD]
                own(V.tensor_tensor(y3, PS[:, 4, :].rearrange("p (h d) -> p h d", h=HB),
                                    c("xi").unsqueeze(2).to_broadcast(per), ALU.mult), G("b_yread"))
                if t < T - 1:
                    kv = PS[:, 5, :].rearrange("p (j e) -> p j e", j=4)
                    dve.wait_ge(G("b_kv"), t + 1)
                    if t >= 1:
                        own(V.tensor_tensor(WB["st"], WB["st"], kv, ALU.add))
                        src = WB["st"]
                    else:
                        src = kv
                    own(V.tensor_tensor(WB["st"], src, c("carry").rearrange("p (j e) -> p j e", j=4), ALU.mult),
                        G("b_state"))
                own(V.tensor_reduce(small[:, 24:32], y3, X_AXIS, ALU.add))
                own(V.tensor_scalar(small[:, 24:32], small[:, 24:32], 1.0 / HD, None, ALU.mult))
                own(V.tensor_tensor(y3, y3, small[:, 24:32].unsqueeze(2).to_broadcast(per), ALU.subtract))
                own(V.tensor_tensor(sq3, y3, y3, ALU.mult))
                own(V.tensor_reduce(small[:, 24:32], sq3, X_AXIS, ALU.add))
                own(V.tensor_scalar(small[:, 32:40], small[:, 24:32], 1.0 / HD, EPS, ALU.mult, ALU.add), G("b_ms"))
                dve.wait_ge(G("b_g"), t + 1)
                own(V.tensor_tensor(y, y, WB["g"][:, t % 2], ALU.mult))
                dve.wait_ge(G("b_rs"), t + 1)
                own(V.tensor_tensor(y3, y3, small[:, 40:48].unsqueeze(2).to_broadcast(per), ALU.mult), G("b_out"))

            for q in range(2):
                dve.wait_ge(G(f"st_q{q}"), 16 * (T // 2))
            for t in range(T):
                b_rotate(t)
                spend(B_SPEND[0])
                if t >= 1:
                    b_retain(t - 1)
                    spend(B_SPEND[2])
            b_retain(T - 1)
            dve.wait_ge(G("c_clear"), 1)
            own(V.tensor_scalar(WC["bias01"][:, 192:256], c("unseen"), NEG_LOGIT, None, ALU.mult))

            def negated_logits(u):
                i = u // HA
                K = cols_of(i)
                bias = WC["bias01"][:, 256 - K:256] if i < FIRST_SCORED else ACC[:, ACC_OFF[i]:ACC_OFF[i] + K]
                b = 2 * (u % 2)
                dve.wait_ge(G("c_qk"), u + 1)
                if u >= 3:
                    pi, ph = divmod(u - 3, HA)
                    dve.wait_ge(G("c_tr"), pt_index(pi, ph, groups(pi) - 1) + 1)
                own.go(V.tensor_tensor_reduce(
                    out=WC["S"][:, u % 3, 0:K], in0=PS[:, b:b + 2, :].rearrange("p b c -> p (b c)")[:, 0:K],
                    in1=bias, scale=-HD ** -0.5, scalar=3.0e38, op0=ALU.add, op1=ALU.min,
                    accum_out=nmax[:, u % 4:u % 4 + 1]), G("c_soft"))

            negated_logits(0)
            negated_logits(1)
            for kind, i in order:
                if kind == "heads":
                    i, lo, hi = i
                    if i == T - 2 and lo == 0:
                        for _ in last_pieces:
                            pass
                    for u in range(HA * i + lo + 2, min(HA * i + hi + 2, HA * T)):
                        negated_logits(u)
                    spend(HEADS_SPEND[i], last_pieces)
                if kind == "mix" and i == 0:
                    sum_up(3)
                if kind == "late":
                    shape, part, at = LATE[i]
                    sum_up(2 * i + 2)
                    for h in range(2):
                        n7 = at7[("late", i, h)]
                        dve.wait_ge(G("b7_ready"), n7 + 1)
                        if shape == "row":
                            if at == 0:
                                dve.wait_ge(G("ld_c"), 16 * 2)
                            if at == 1:
                                dve.wait_ge(G("ld_gt2"), 16)
                            dst = (WC["gt1"] if at == 0 else gt2)[:, 512 * h:512 * h + 512]
                            own(V.tensor_tensor(dst, PS[:, 7, :], dst, ALU.add), G("b7_free"))
                        else:
                            own_columns(7, late_sum[2 * i + h], at, h, G("b7_free"))
                            if at == 2 and h == 1:
                                own(V.scalar_tensor_tensor(mod[:, 2, :], mod[:, 2, :], 1.0, gc[:, 1, :], ALU.add,
                                                           ALU.mult))
                if kind == "rows":
                    dve.wait_ge(G("c_exp"), HA * (i + 1))
                    own(V.reciprocal(ssum[:, i % 2, :], ssum[:, i % 2, :]))
                    dve.wait_ge(G("c_pv"), pt_index(i, HA - 1, groups(i) - 1) + 1)
                    if i >= 1:
                        dve.wait_ge(G("c_ytr"), i)
                    own(V.tensor_tensor(WC["y"].rearrange("p (h d) -> p h d", h=HA),
                                        PS[:, 6, :].rearrange("p (h d) -> p h d", h=HA),
                                        ssum[:, i % 2, :].unsqueeze(2).to_broadcast([P, HA, HD]), ALU.mult), G("c_y"))
                if kind == "mix":
                    dve.wait_ge(G("ld_xr"), 16 * (i + 1))
                    if i >= 1:
                        dve.wait_ge(G("c_htr"), i)
                        dve.wait_ge(G("st_xn"), 16 * i)
                    for h in range(2):
                        spend(MIX_SPEND, last_pieces)
                        n7 = at7[("mix", i, h)]
                        part = slice(512 * h, 512 * h + 512)
                        dve.wait_ge(G("b7_ready"), n7 + 1)
                        own(V.tensor_tensor(WC["sq"][:, part], PS[:, 7, :], WC["gt1"][:, part], ALU.mult),
                            G("b7_free"))
                        own(V.tensor_tensor(WC["x"][:, part], WC["x"][:, part], WC["sq"][:, part], ALU.add),
                            G("c_x1") if h else None)
                if kind == "norm":
                    dve.wait_ge(G("c_sq"), i + 1)
                    own(V.tensor_scalar(small[:, 48:49], small[:, 52:53], 1.0 / D, EPS, ALU.mult, ALU.add),
                        G("c_ms"))
                    dve.wait_ge(G("c_rs"), i + 1)
                    own(V.tensor_scalar(WC["sq"], WC["x"], small[:, 49:50], None, ALU.mult), G("c_xn"))
                if kind == "route":
                    dve.wait_ge(G("c_htr"), i + 1)
                    modulate_all(WC["h2T"], 4, 1, G("c_h2"))
                    dve.wait_ge(G("b7_ready"), at7[("route", i, 0)] + 1)
                    own(V.tensor_copy(L[:, i, :], PS[:, 7, 0:36]), G("b7_free"))
            dve.wait_ge(G("st_x1"), 16 * T)
            dve.wait_ge(G("st_xn"), 16 * T)
            q8 = [P, T, 8]
            desc = c("desc")

            def largest(values, n, top, first, scratch):
                own(V.tensor_reduce(top, values, X_AXIS, ALU.max))
                own(V.tensor_tensor(scratch, values, top.unsqueeze(2).to_broadcast([P, T, n]), ALU.is_equal))
                own(V.tensor_tensor(scratch, scratch, desc[:, 8 - n:8].unsqueeze(1).to_broadcast([P, T, n]),
                                    ALU.mult))
                own(V.tensor_reduce(WR["m"], scratch, X_AXIS, ALU.max))
                own(V.tensor_tensor(first, scratch, WR["m"].unsqueeze(2).to_broadcast([P, T, n]), ALU.is_equal))

            Lg = L[:, :, 0:NG]
            largest(Lg, NG, WR["gm"], WR["G"], WR["cg"])
            own(V.tensor_tensor(WR["cg"], Lg, WR["gm"].unsqueeze(2).to_broadcast([P, T, NG]), ALU.subtract))
            own(V.tensor_tensor(WR["tmp"].rearrange("p t (g e) -> p t g e", g=NG),
                                L[:, :, NG:36].rearrange("p t (g e) -> p t g e", g=NG),
                                WR["G"].unsqueeze(3).to_broadcast([P, T, NG, EPG]), ALU.mult))
            own(V.tensor_reduce(WR["f"], WR["tmp"].rearrange("p t (g e) -> p t e g", g=NG), X_AXIS, ALU.add))
            largest(WR["f"], 8, WR["t1"], WR["o1"], WR["ca"])
            own(V.scalar_tensor_tensor(WR["f2"], WR["o1"], TAKEN, WR["f"], ALU.mult, ALU.add))
            largest(WR["f2"], 8, WR["t2"], WR["o2"], WR["ca"])
            own(V.tensor_tensor(WR["e2x"], WR["t2"], WR["t1"], ALU.subtract), G("r_arg"))
            dve.wait_ge(G("r_exp"), 1)
            own(V.tensor_reduce(WR["gm"], WR["cg"], X_AXIS, ALU.add))
            own(V.tensor_scalar(WR["t1"], WR["e2x"], 1.0, None, ALU.add))
            own(V.tensor_tensor(WR["t1"], WR["t1"], WR["gm"], ALU.mult))
            own(V.reciprocal(sw[:, 0, :], WR["t1"]))
            own(V.tensor_tensor(sw[:, 1, :], sw[:, 0, :], WR["e2x"], ALU.mult))
            for e, o in (("e1", "o1"), ("e2", "o2")):
                own(V.tensor_tensor(WR[e].rearrange("p t (g e) -> p t g e", g=NG),
                                    WR["G"].unsqueeze(3).to_broadcast([P, T, NG, EPG]),
                                    WR[o].unsqueeze(2).to_broadcast([P, T, NG, EPG]), ALU.mult))
            own(V.tensor_tensor(WR["A"], WR["e1"], WR["e2"], ALU.add))
            own(V.memset(WR["pre"][:, 0], 0.0))
            for t in range(1, T):
                own(V.tensor_tensor(WR["pre"][:, t], WR["pre"][:, t - 1], WR["A"][:, t - 1], ALU.add))
            own(V.tensor_tensor(WR["cnt"], WR["pre"][:, T - 1], WR["A"][:, T - 1], ALU.add), G("r_dve"))
            dve.wait_ge(G("r_pe"), 1)
            rank = PS[:, 0, 0:256].rearrange("p (t e) -> p t e", t=T)
            own(V.tensor_copy(WR["cnt"], PS[:, 1, 0:NE]))
            ends, nb = WR["ends"], WR["nb"]
            own(V.tensor_scalar(nb, WR["cnt"], 0.0, None, ALU.is_gt))
            for k in range(1, T):
                own(V.scalar_tensor_tensor(nb, WR["cnt"], float(P * k), nb, ALU.is_gt, ALU.add))
            own(V.tensor_copy(ends[:, 0], nb))
            for n, step in enumerate((1, 2, 4, 8, 16)):
                src, dst = ends[:, n % 2], ends[:, (n + 1) % 2]
                own(V.tensor_copy(dst[:, 0:step], src[:, 0:step]))
                own(V.tensor_tensor(dst[:, step:NE], src[:, step:NE], src[:, 0:NE - step], ALU.add))
            end = ends[:, 1]
            it2 = WR["it"][0:1, 0:MAX_ITEMS * NE].rearrange("p (i e) -> p i e", i=MAX_ITEMS)
            own(V.tensor_tensor(it2, end[0:1].unsqueeze(1).to_broadcast([1, MAX_ITEMS, NE]),
                                c("iota")[0:1, 0:MAX_ITEMS].unsqueeze(2).to_broadcast([1, MAX_ITEMS, NE]),
                                ALU.is_le))
            own(V.tensor_reduce(WR["ef"][0:1, 0:MAX_ITEMS], it2, X_AXIS, ALU.add))
            own(V.tensor_scalar(WR["ef"][0:1, 0:MAX_ITEMS], WR["ef"][0:1, 0:MAX_ITEMS], float(NE - 1), None,
                                ALU.min))
            own(V.tensor_scalar(WR["h"][0:1, 0:MAX_ITEMS // 2], c("even")[0:1, :], end[0:1, NE - 1:NE], None,
                                ALU.is_lt))
            own(V.tensor_reduce(WR["h"][0:1, 32:33], WR["h"][0:1, 0:MAX_ITEMS // 2], X_AXIS, ALU.add))
            own(V.tensor_scalar(WR["h"][0:1, 32:33], WR["h"][0:1, 32:33], (PEELED + 1) / 2, None, ALU.subtract))
            own(V.tensor_copy(items[0:1, 0:MAX_ITEMS], WR["ef"][0:1, 0:MAX_ITEMS]))
            own(V.tensor_copy(items[0:1, 63:64], WR["h"][0:1, 32:33]), G("r_items"))
            own(V.tensor_tensor(WR["start"], end, nb, ALU.subtract))
            own(V.scalar_tensor_tensor(WR["V"], WR["start"].unsqueeze(1).to_broadcast([P, T, NE]), float(P), rank,
                                       ALU.mult, ALU.add))
            for e, name in enumerate(("e1", "e2")):
                own(V.tensor_tensor(WR["tmp"], WR[name], WR["V"], ALU.mult))
                own(V.tensor_reduce(WR["row"][:, e], WR["tmp"], X_AXIS, ALU.add))
                own(V.tensor_copy(srow[:, e, :], WR["row"][:, e]))
            row16 = WR["row"].rearrange("p e t -> p (e t)")
            q16 = WR["q"].rearrange("p e t -> p (e t)")
            r16 = WR["r"].rearrange("p e t -> p (e t)")
            it3 = WR["it"][:, 0:768].rearrange("p (r k) -> p r k", r=16)
            own(V.tensor_scalar(WR["h48"], c("iota")[:, 1:49], float(P), None, ALU.mult))
            own(V.tensor_tensor(it3, row16.unsqueeze(2).to_broadcast([P, 16, 48]),
                                WR["h48"].unsqueeze(1).to_broadcast([P, 16, 48]), ALU.is_ge))
            own(V.tensor_reduce(q16, it3, X_AXIS, ALU.add))
            own(V.scalar_tensor_tensor(r16, q16, -float(P), row16, ALU.mult, ALU.add))
            for n in range(2 * T):
                e, t = divmod(n, T)
                if n >= 2:
                    dve.wait_ge(G("r_acc"), n - 1)
                own.go(V.tensor_scalar(WR["ohp"][:, n % 2], c("iota"), WR["r"][:, e, t:t + 1], None, ALU.is_equal))
                own.go(V.tensor_scalar(WR["ohi"][:, n % 2], c("iota")[:, 0:64], WR["q"][:, e, t:t + 1],
                                       c("token")[:, t:t + 1], ALU.is_equal, ALU.mult), G("r_oh"))
            own.wait()
            dve.wait_ge(G("r_acc"), 2 * T)
            own(V.tensor_copy(tbl[:, :], PS[:, 2, 0:TBL]), G("r_done"))

            rounds = nc.vector.value_load(items[0:1, 63:64], min_val=1, max_val=MOST_ROUNDS)

            def low(i, s, q):
                n, slot = place(i, s, q)
                dve.wait_ge(G("m_hi"), n + 1)
                V.tensor_tensor(wlo[:, slot], raw[:, q], whi[:, slot].bitcast(F32), ALU.subtract)\
                    .then_inc(G("m_lo"), 1)

            def turned_rows(i):
                dve.wait_ge(G("m_xtr"), i + 1)
                if not known(i, 1):
                    dve.wait_ge(G("m_xlo"), i)
                for k, ins in enumerate(modulate(WM["xT"], 0, 1)):
                    ins.then_inc(G("m_xm") if k == KD - 1 else G("m_part"), 1)

            def low_hidden(i):
                dve.wait_ge(G("m_hhi"), i + 1)
                V.tensor_tensor(hlo[:, :, :], PS[:, 4, :].rearrange("p (k n) -> p k n", k=KF),
                                hhi[:, :, :].bitcast(F32), ALU.subtract).then_inc(G("m_hlo"), 1)

            def down_half(i, s, after):
                dve.wait_ge(G("m_used"), after + 1)
                dve.wait_ge(G(f"st_y{s}"), 8 * (i - s) + 64)
                V.tensor_copy(WM["Y"][:, s, 512:1024], PS[:, 6, :]).then_inc(G("m_yd"), 1)

            def step(i, s, last):
                if not known(i, 1):
                    low_hidden(i - 1)
                low(i, s, UP[0])
                if not last:
                    turned_rows(i + 1)
                low(i, s, UP[1])
                if not last:
                    low(i + 1, 1 - s, GATE[0])
                if not known(i, 1):
                    down_half(i - 1, 1 - s, place(i, s, DOWN[1])[0])
                if not last:
                    low(i + 1, 1 - s, GATE[1])
                low(i + 1, TAIL if last else 1 - s, DOWN[0])
                dve.wait_ge(G("m_silu"), i + 1)
                dve.wait_ge(G("m_used"), place(i, s, UP[1])[0] + 1)
                V.tensor_tensor(WM["h"], WM["hs"], PS[:, 3, :], ALU.mult).then_inc(G("m_h"), 1)
                low(i + 1, TAIL if last else 1 - s, DOWN[1])

            turned_rows(0)
            for q in GATE:
                low(0, 0, q)
            steps(dve, rounds, step)
            low_hidden(count(rounds) - 1)
            down_half(count(rounds) - 1, 1, place(count(rounds), TAIL, DOWN[1])[0])
            dve.wait_ge(G("m_end"), 1)
            dve.wait_ge(G("ld_gf"), 16)
            def f_finish(t):
                xf = WF["x"][t % NF]
                dve.wait_ge(G("f_rs"), t + 1)
                own(V.scalar_tensor_tensor(xf, xf, f_rs[t % 2], WF["gf"], ALU.mult, ALU.mult), G("f_out"))

            for t in range(T):
                s = t % 2
                xf, y1, y2 = WF["x"][t % NF], WF["y1"][t % NF], WF["y2"][t % NF]
                dve.wait_ge(G(f"f_y{t % NF}"), 32 * (t // NF + 1))
                dve.wait_ge(G("f_scaled"), t + 1)
                own(V.scalar_tensor_tensor(y1, y2, sw[:, 1, t:t + 1], y1, ALU.mult, ALU.add))
                own(V.tensor_tensor(y1, y1, gt2, ALU.mult))
                dve.wait_ge(G(f"ld_x{t}"), 32)
                own(V.tensor_tensor(xf, xf, y1, ALU.add), G("f_sum"))
                if t >= 1:
                    f_finish(t - 1)
                dve.wait_ge(G("f_sq"), t + 1)
                own(V.tensor_scalar(f_ms[s], small[:, 53 + s:54 + s], 1.0 / D, EPS, ALU.mult, ALU.add), G("f_ms"))
            f_finish(T - 1)

        @block.tensor
        def _(pe):
            mm, tr = nc.tensor.matmul, nc.tensor.transpose

            def turn_rows(rows, bank):
                for k in range(KD):
                    last = tr(PS[:, bank + k // 4, P * (k % 4):P * (k % 4) + P], rows[:, P * k:P * k + P], ident)
                return last

            pe.wait_ge(G("ld_const"), 16 * 5)
            pe.wait_ge(G("pool_ones"), 1)
            for t in range(T):
                pe.wait_ge(G("xn_ready"), t + 1)
                if t >= 2:
                    pe.wait_ge(G("hT_raw"), t - 1)
                turn_rows(xall[:, t, :], 4 + 2 * (t % 2)).then_inc(G("xt_ready"), 1)
            for s in range(2):
                pe.wait_ge(G("mac_done"), s + 1)
                for h in range(2):
                    last = mm(PS[:, 2 * s + h, :], ones[:, :], W0["mac"][:, s, 512 * h:512 * h + 512], start=True,
                              stop=True)
                last.then_inc(G("pe_cols"), 1)

            def a_turn(m):
                u = turned[m]
                pe.wait_ge(G("a_rot"), m + 1)
                if m >= 2:
                    pe.wait_ge(G("a_evac"), m - 1)
                n = 1 if CHUNKS_A[u // T][0] == "kiwi" else 4
                for k in range(n):
                    last = tr(PS[:, 4 + m % 2, P * k:P * k + P], WA["tmp"][:, m % 3, P * k:P * k + P], ident)
                last.then_inc(G("a_tr"), 1)

            def a_project(chunks):
                m = turned.index(chunks[0] * T)
                m0 = m
                for n in chunks:
                    name, _, w = CHUNKS_A[n]
                    pe.wait_ge(G(f"ld_w{n % 2}"), 16 * (n // 2 + 1))
                    for t in range(T):
                        u = n * T + t
                        if n == 0:
                            pe.wait_ge(G("hT_ready"), 1 + t // 4)
                        if u >= 4:
                            pe.wait_ge(G("a_copied"), u - 3)
                        for k in range(KD):
                            last = mm(PS[:, u % 4, 0:w], hT[:, k, tile(t)], ring[n % 2][:, k, 0:w], start=(k == 0),
                                      stop=(k == KD - 1))
                        last.then_inc(G("a_proj"), 1)
                        if name != "va":
                            if m > m0:
                                a_turn(m - 1)
                            m += 1
                        elif t == 0:
                            a_turn(m - 1)
                if name != "va":
                    a_turn(m - 1)

            a_project(range(NA1))
            pe.wait_ge(G("a_copied"), NA1 * T)
            pe.wait_ge(G("a_evac"), TURN1)
            for u in range(NU):
                i, h = FIRST_SCORED + u // NIH, u % NIH
                K = cols_of(i)
                if u >= 3:
                    pe.wait_ge(G("sc_relu"), u - 2)
                for b in range((K + 511) // 512):
                    w = min(512, K - 512 * b)
                    last = mm(PS[:, 2 * (u % 3) + b, 0:w], qiT[:, h // 2, tile(i)], kiBD[:, h % 2, 512 * b:512 * b + w],
                              start=True, stop=True)
                last.then_inc(G("sc_ready"), 1)
            pe.wait_ge(G("sc_relu"), NU)
            a_project(range(NA1, NA))
            pe.wait_ge(G("a_copied"), UA)
            pe.wait_ge(G("a_evac"), NTURN)

            def b_retain(t):
                q_, k_, v_ = WB["qA"][:, t % 2], WB["kA"][:, t % 2], WB["v"][:, t % 2]
                pe.wait_ge(G("b_qr"), t + 1)
                if t >= 1:
                    pe.wait_ge(G("b_yread"), t)
                for j in range(4):
                    last = tr(PS[:, 4, P * j:P * j + P], q_[:, P * j:P * j + P], ident)
                last.then_inc(G("b_trq"), 1)
                pe.wait_ge(G("b_kr"), t + 1)
                if t >= 1:
                    pe.wait_ge(G("b_state"), t)
                for j in range(4):
                    last = tr(PS[:, 5, P * j:P * j + P], k_[:, P * j:P * j + P], ident)
                last.then_inc(G("b_trk"), 1)
                pe.wait_ge(G("b_qbd"), t + 1)
                pe.wait_ge(G("b_kT"), t + 1)
                if t >= 1:
                    pe.wait_ge(G("b_sm"), t)
                for j in range(4):
                    last = mm(PS[:, 6 + j // 2, 256 * (j % 2):256 * (j % 2) + 256], WB["kT"][:, j, :],
                              WB["qBD"][:, j].rearrange("p h n -> p (h n)"), start=True, stop=True)
                last.then_inc(G("b_s"), 1)
                pe.wait_ge(G("b_v"), t + 1)
                if t < T - 1:
                    for j in range(4):
                        last = mm(PS[:, 5, P * j:P * j + P], k_[:, P * j:P * j + P], v_[:, P * j:P * j + P],
                                  start=True, stop=True)
                    last.then_inc(G("b_kv"), 1)
                pe.wait_ge(G("b_sm"), t + 1)
                for h in range(HB):
                    o = PS[:, 4, HD * h:HD * h + HD]
                    if t >= 1:
                        mm(o, WB["qBD"][:, h // 2, h % 2, :], WB["st"][:, h // 2, HD * (h % 2):HD * (h % 2) + HD],
                           start=True, stop=False)
                    last = mm(o, WB["S"][:, h, :], v_[:, HD * h:HD * h + HD], start=(t == 0), stop=True)
                last.then_inc(G("b_y"), 1)

            for t in range(T):
                for k in range(4):
                    if t == 0:
                        pe.wait_ge(G(f"ld_wb{k}"), 16)
                    else:
                        pe.wait_ge(G(("b_qsplit", "b_ksplit", "b_v", "b_g")[k]), t)
                    for d in range(KD):
                        last = mm(PS[:, k, :], hT[:, d, tile(t)], wb[k][:, d, :], start=(d == 0), stop=(d == KD - 1))
                    last.then_inc(G("b_proj"), 1)
                if t >= 1:
                    b_retain(t - 1)
            b_retain(T - 1)
            for name in ("b_qsplit", "b_ksplit", "b_v", "b_g", "b_yread", "b_sm"):
                pe.wait_ge(G(name), T)
            pe.wait_ge(G("b_state"), T - 1)

            def bank7(use):
                if at7[use] >= 1:
                    pe.wait_ge(G("b7_free"), at7[use])

            def query_keys(u):
                i, h = divmod(u, HA)
                K = cols_of(i)
                if h == 0:
                    pe.wait_ge(G(f"ld_q{i % 2}"), 32 * (i // 2 + 1))
                if u >= 2:
                    pe.wait_ge(G("c_soft"), u - 1)
                for b in range((K + 511) // 512):
                    w = min(512, K - 512 * b)
                    last = mm(PS[:, 2 * (u % 2) + b, 0:w], WC["qBD"][i % 2][:, h // 2, h % 2, :],
                              kaT[:, h // 2, 512 * b:512 * b + w], start=True, stop=True)
                last.then_inc(G("c_qk"), 1)

            def values(i, h, g):
                n = pt_index(i, h, g)
                pe.wait_ge(G("c_pt"), n + 1)
                if h == 0 and g == 0 and i >= 1:
                    pe.wait_ge(G("c_y"), i)
                for b in range(4 * g, min(4 * g + 4, i + 1)):
                    last = mm(PS[:, 6, HD * h:HD * h + HD], WC["PT"][:, n % 2, P * (b % 4):P * (b % 4) + P],
                              va[:, b, HD * h:HD * h + HD], start=(b == 0), stop=(b == i))
                last.then_inc(G("c_pv"), 1)

            for kind, i in order:
                if kind == "heads":
                    i, lo, hi = i
                    if i == 0 and lo == 0:
                        query_keys(0)
                        query_keys(1)
                    todo = None
                    for h in range(lo, hi):
                        if HA * i + h + 2 < HA * T:
                            query_keys(HA * i + h + 2)
                        for g in range(groups(i)):
                            n = pt_index(i, h, g)
                            pe.wait_ge(G("c_exp"), HA * i + h + 1)
                            if n >= 2:
                                pe.wait_ge(G("c_pt"), n - 1)
                            for b in range(4 * g, min(4 * g + 4, i + 1)):
                                last = tr(PS[:, 4 + n % 2, P * (b % 4):P * (b % 4) + P],
                                          WC["S"][:, (HA * i + h) % 3, P * b:P * b + P], ident)
                            last.then_inc(G("c_tr"), 1)
                            if todo:
                                values(*todo)
                            todo = (i, h, g)
                    values(*todo)
                if kind == "late":
                    for h in range(2):
                        pe.wait_ge(G("late_sum"), 2 * i + h + 1)
                        bank7(("late", i, h))
                        mm(PS[:, 7, :], ones[:, :], late_sum[(2 * i + h) % 6], start=True, stop=True)\
                            .then_inc(G("b7_ready"), 1)
                if kind == "mix":
                    pe.wait_ge(G("c_y"), i + 1)
                    pe.wait_ge(G("ld_yb"), 16 * (i + 1))
                    for k in range(8):
                        src = WC["y"] if k < 4 else WC["yb"]
                        last = tr(PS[:, 4 + k // 4, P * (k % 4):P * (k % 4) + P],
                                  src[:, P * (k % 4):P * (k % 4) + P], ident)
                    last.then_inc(G("c_ytr"), 1)
                    pe.wait_ge(G("c_yT"), i + 1)
                    pe.wait_ge(G("ld_wo"), 16)
                    for h in range(2):
                        bank7(("mix", i, h))
                        for k in range(KD):
                            last = mm(PS[:, 7, :], WC["yT"][:, k, :], wo[:, k, 512 * h:512 * h + 512], start=(k == 0),
                                      stop=(k == KD - 1))
                        last.then_inc(G("b7_ready"), 1)
                if kind == "route":
                    pe.wait_ge(G("c_xn"), i + 1)
                    turn_rows(WC["sq"], 4).then_inc(G("c_htr"), 1)
                    pe.wait_ge(G("c_h2"), i + 1)
                    bank7(("route", i, 0))
                    pe.wait_ge(G("ld_c"), 16 * 2)
                    for k in range(KD):
                        last = mm(PS[:, 7, 0:36], WC["h2T"][:, k, :], WC["wr"][:, 36 * k:36 * k + 36],
                                  start=(k == 0), stop=(k == KD - 1))
                    last.then_inc(G("b7_ready"), 1)
            pe.wait_ge(G("r_dve"), 1)
            rank = PS[:, 0, 0:256]
            mm(rank, c("before"), WR["A"].rearrange("p t e -> p (t e)"), start=True, stop=False)
            mm(rank, ones[:, :], WR["pre"].rearrange("p t e -> p (t e)"), start=False, stop=True)
            mm(PS[:, 1, 0:NE], ones[:, :], WR["cnt"], start=True, stop=True).then_inc(G("r_pe"), 1)
            for n in range(2 * T):
                pe.wait_ge(G("r_oh"), n + 1)
                mm(PS[:, 2, 0:64], WR["ohp"][:, n % 2], WR["ohi"][:, n % 2], start=(n == 0),
                   stop=(n == 2 * T - 1)).then_inc(G("r_acc"), 1)
            pe.wait_ge(G("r_done"), 1)
            rounds = nc.tensor.value_load(items[0:1, 63:64], min_val=1, max_val=MOST_ROUNDS)
            def turn(i, s):
                pe.wait_ge(G(f"ld_rows{s}"), 8 * (i - s) + 16)
                if not known(i, 1):
                    pe.wait_ge(G("m_xm"), i)
                turn_rows(WM["Xg"][:, s], 0).then_inc(G("m_xtr"), 1)

            def split_product(out_, x_hi, x_lo, w_hi, w_lo, first, final):
                mm(out_, x_hi, w_hi, start=first, stop=False)
                mm(out_, x_hi, w_lo, start=False, stop=False)
                return mm(out_, x_lo, w_hi, start=False, stop=final)

            def rows_half(i, s, q, bank):
                n, slot = place(i, s, q)
                pe.wait_ge(G("m_lo"), n + 1)
                h = q % 2
                for k in range(4):
                    part = slice(512 * k, 512 * k + 512)
                    last = split_product(PS[:, bank, :], xhi[:, s, 4 * h + k], xlo[:, s, 4 * h + k],
                                         whi[:, slot, part], wlo[:, slot, part], h == 0 and k == 0, h == 1 and k == 3)
                last.then_inc(G("m_used"), 1)

            def turn_hidden(i):
                pe.wait_ge(G("m_h"), i + 1)
                for k in range(KF):
                    last = tr(PS[:, 4, P * k:P * k + P], WM["h"][:, P * k:P * k + P], ident)
                last.then_inc(G("m_htr"), 1)

            def down(i, s):
                pe.wait_ge(G("m_hlo"), i)
                if not known(i, 2):
                    pe.wait_ge(G("m_ya"), i - 1)
                    pe.wait_ge(G("m_yd"), i - 1)
                for q in DOWN:
                    n, slot = place(i, s, q)
                    pe.wait_ge(G("m_lo"), n + 1)
                    for h in range(2):
                        for k in range(2):
                            part = slice(1024 * k + 512 * h, 1024 * k + 512 * h + 512)
                            kk = 2 * (q % 2) + k
                            last = split_product(PS[:, 5 + h, :], hhi[:, kk], hlo[:, kk], whi[:, slot, part],
                                                 wlo[:, slot, part], kk == 0, kk == KF - 1)
                    last.then_inc(G("m_used"), 1)

            def step(i, s, last):
                pe.wait_ge(G("m_xlo"), i + 1)
                if not known(i, 1):
                    pe.wait_ge(G("m_silu"), i)
                rows_half(i, s, GATE[0], 2)
                if not known(i, 1):
                    turn_hidden(i - 1)
                rows_half(i, s, GATE[1], 2)
                if not last:
                    turn(i + 1, 1 - s)
                if not known(i, 1):
                    down(i, s)
                    pe.wait_ge(G("m_h"), i)
                for q in UP:
                    rows_half(i, s, q, 3)

            turn(0, 0)
            steps(pe, rounds, step)
            turn_hidden(count(rounds) - 1)
            down(count(rounds), TAIL)


_OUT = "out_dram"


def kernel(**inputs):
    import concourse.bacc as _bacc
    from concourse.bass_utils import run_bass_kernel_spmd as _run

    a = {k: np.asarray(v) for k, v in inputs.items()}

    def cols(v):
        return v.reshape(KD, P).T

    b = a["b_ada"][0].reshape(6, D)
    wr = np.concatenate([a["w_router_group"][0], a["w_router_expert"][0].transpose(1, 0, 2).reshape(D, NE)], 1)
    arrays = {
        "x": a["x"][0],
        "ccol": cols(a["c"][0]),
        "pos": a["positions"][0].reshape(T, P).T,
        "w_ada": a["w_ada"][0],
        "b_cols": np.stack([cols(b[1]), cols(b[0]), cols(b[4]), cols(b[3])], 1),
        "b_gt1": np.broadcast_to(b[2], (P, D)),
        "b_gt2": np.broadcast_to(b[5], (P, D)),
        "g_cols": np.stack([cols(a["g_norm_mix"][0]), cols(a["g_norm_ffn"][0])], 1),
        "g_final": np.broadcast_to(a["g_norm_final"], (P, D)),
        "w_in": a["w_in"][0],
        "w_o": a["w_o"][0],
        "w_router": wr.reshape(KD, P, 36).transpose(1, 0, 2).reshape(P, KD * 36),
        "w_up": a["w_up"][0],
        "w_gate": a["w_gate"][0],
        "w_down": a["w_down"][0],
        "const": CONST,
    }
    nc = _bacc.Bacc("TRN2", target_bir_lowering=False, num_devices=1)
    given, args = {}, {}
    for name, v in arrays.items():
        v = np.ascontiguousarray(v)
        given[f"in_{name}"] = v
        args[name] = nc.dram_tensor(f"in_{name}", v.shape, mybir.dt.from_np(v.dtype), kind="ExternalInput").ap()
    args["out"] = nc.dram_tensor(_OUT, (S, D), F32, kind="ExternalOutput").ap()
    block_kernel(nc, **args)
    r = _run(nc, [given], core_ids=[0])
    return r.results[0][_OUT].reshape(1, S, D)
```
